# Optimizing a Trainium2 kernel written in Bass

```python
import math
import jax, jax.numpy as jnp
from jax import lax
import numpy as np

D_MODEL = 1024
BATCH = 1
SEQ = 512
DEPTH = 2

N_MIXERS = 2
ROPE_THETA = 10000.0
EPS = 1e-6
Q_BLOCK = 128
NEG_INF = -1e30
MAX_POS_OFFSET = 1024
DA_HEAD_DIM = 64
DA_HEADS = D_MODEL // (2 * DA_HEAD_DIM)
MLA_HEADS = 16
MLA_NOPE = 64
MLA_ROPE = 32
MLA_V = 64
MLA_Q_RANK = 384
MLA_KV_RANK = 256
N_GROUPS = 4
EXPERTS_PER_GROUP = 8
TOP_K = 2
EXPERT_FF = 256

kernel_name = "hybrid_diffattn_mla_hmoe_adaln"

def rms_norm(x, g):
    xf = x.astype(jnp.float32)
    y = xf * lax.rsqrt(jnp.mean(xf * xf, axis=-1, keepdims=True) + EPS)
    return (y * g.astype(jnp.float32)).astype(x.dtype)

def rope_tables(positions, dim):
    inv_freq = ROPE_THETA ** (-jnp.arange(0, dim, 2, dtype=jnp.float32) / dim)
    ang = positions.astype(jnp.float32)[..., None] * inv_freq
    return jnp.cos(ang), jnp.sin(ang)

def apply_rope(x, cos, sin):
    extra = x.ndim - 3
    shp = cos.shape[:2] + (1,) * extra + cos.shape[-1:]
    cos = cos.reshape(shp)
    sin = sin.reshape(shp)
    xf = x.astype(jnp.float32)
    x1, x2 = jnp.split(xf, 2, axis=-1)
    return jnp.concatenate([x1 * cos - x2 * sin, x2 * cos + x1 * sin], axis=-1).astype(x.dtype)

def modulate(x, shift, scale):
    return x * (1.0 + scale[:, None, :]) + shift[:, None, :]

def causal_mask(start, q_len, k_len):
    qpos = start + jnp.arange(q_len)
    kpos = jnp.arange(k_len)
    return kpos[None, :] <= qpos[:, None]

def diff_attention(h, cos, sin, w_qkv, q_norm, k_norm, lq1, lk1, lq2, lk2, subln, w_o, lambda_init):
    B, S, _ = h.shape
    H, dh = DA_HEADS, DA_HEAD_DIM
    q, k, v = jnp.split(h @ w_qkv, 3, axis=-1)
    q = q.reshape(B, S, H, 2, dh)
    k = k.reshape(B, S, H, 2, dh)
    v = v.reshape(B, S, H, 2 * dh)
    q = apply_rope(rms_norm(q, q_norm), cos, sin)
    k = apply_rope(rms_norm(k, k_norm), cos, sin)
    lam = (jnp.exp(jnp.sum(lq1.astype(jnp.float32) * lk1.astype(jnp.float32)))
           - jnp.exp(jnp.sum(lq2.astype(jnp.float32) * lk2.astype(jnp.float32))) + lambda_init)
    scale = dh ** -0.5
    outs = []
    for j in range(S // Q_BLOCK):
        s0 = j * Q_BLOCK
        L = s0 + Q_BLOCK
        s = jnp.einsum('bqhcd,bkhcd->bhcqk', q[:, s0:L], k[:, :L],
                       preferred_element_type=jnp.float32) * scale
        p = jax.nn.softmax(jnp.where(causal_mask(s0, Q_BLOCK, L), s, NEG_INF), axis=-1)
        a = p[:, :, 0] - lam * p[:, :, 1]
        outs.append(jnp.einsum('bhqk,bkhd->bqhd', a.astype(v.dtype), v[:, :L]))
    o = jnp.concatenate(outs, axis=1)
    o = rms_norm(o, subln) * (1.0 - lambda_init)
    return o.reshape(B, S, H * 2 * dh) @ w_o

def mla_attention(h, cos, sin, w_in, q_a_norm, kv_a_norm, w_uq, w_ukv,
                  q_nope_norm, q_pe_norm, k_nope_norm, k_pe_norm, w_o):
    B, S, _ = h.shape
    H = MLA_HEADS
    lat = h @ w_in
    cq = lat[..., :MLA_Q_RANK]
    ckv = lat[..., MLA_Q_RANK:MLA_Q_RANK + MLA_KV_RANK]
    k_pe = lat[..., MLA_Q_RANK + MLA_KV_RANK:]
    q = (rms_norm(cq, q_a_norm) @ w_uq).reshape(B, S, H, MLA_NOPE + MLA_ROPE)
    kv = (rms_norm(ckv, kv_a_norm) @ w_ukv).reshape(B, S, H, MLA_NOPE + MLA_V)
    q_nope = rms_norm(q[..., :MLA_NOPE], q_nope_norm)
    q_pe = apply_rope(rms_norm(q[..., MLA_NOPE:], q_pe_norm), cos, sin)
    k_nope = rms_norm(kv[..., :MLA_NOPE], k_nope_norm)
    v = kv[..., MLA_NOPE:]
    k_pe = apply_rope(rms_norm(k_pe, k_pe_norm), cos, sin)
    scale = (MLA_NOPE + MLA_ROPE) ** -0.5
    outs = []
    for j in range(S // Q_BLOCK):
        s0 = j * Q_BLOCK
        L = s0 + Q_BLOCK
        s = (jnp.einsum('bqhd,bkhd->bhqk', q_nope[:, s0:L], k_nope[:, :L], preferred_element_type=jnp.float32)
             + jnp.einsum('bqhr,bkr->bhqk', q_pe[:, s0:L], k_pe[:, :L], preferred_element_type=jnp.float32)) * scale
        p = jax.nn.softmax(jnp.where(causal_mask(s0, Q_BLOCK, L), s, NEG_INF), axis=-1)
        outs.append(jnp.einsum('bhqk,bkhd->bqhd', p.astype(v.dtype), v[:, :L]))
    o = jnp.concatenate(outs, axis=1)
    return o.reshape(B, S, H * MLA_V) @ w_o

def hier_moe(h, w_group, b_group, w_router, b_router, w1, w3, w2):
    B, S, D = h.shape
    G, E = N_GROUPS, EXPERTS_PER_GROUP
    t = h.reshape(B * S, D)
    g_prob = jax.nn.softmax((t @ w_group).astype(jnp.float32), axis=-1)
    g_idx = jnp.argmax(g_prob + b_group.astype(jnp.float32), axis=-1)
    g_gate = jnp.take_along_axis(g_prob, g_idx[:, None], axis=1)
    e_logit = (t @ w_router).astype(jnp.float32).reshape(-1, G, E)
    e_logit = jnp.take_along_axis(e_logit, g_idx[:, None, None], axis=1)[:, 0]
    e_prob = jax.nn.softmax(e_logit, axis=-1)
    _, e_idx = lax.top_k(e_prob + b_router.astype(jnp.float32)[g_idx], TOP_K)
    e_w = jnp.take_along_axis(e_prob, e_idx, axis=1)
    e_w = e_w / jnp.sum(e_w, axis=-1, keepdims=True) * g_gate
    within = jnp.einsum('nk,nke->ne', e_w, jax.nn.one_hot(e_idx, E, dtype=jnp.float32))
    combine = (jax.nn.one_hot(g_idx, G, dtype=jnp.float32)[:, :, None] * within[:, None, :]).astype(t.dtype)
    out = jnp.zeros_like(t)
    for g in range(G):
        a = jnp.einsum('nd,edf->nef', t, w1[g])
        b = jnp.einsum('nd,edf->nef', t, w3[g])
        hid = jax.nn.silu(a) * b * combine[:, g, :, None]
        out = out + jnp.einsum('nef,efd->nd', hid, w2[g])
    return out.reshape(B, S, D)

def setup_inputs(seed: int = 0) -> dict:
    key = jax.random.key(seed)
    ks = iter(jax.random.split(key, 40))
    f32 = jnp.float32
    D = D_MODEL
    n_da = (DEPTH + 1) // 2
    n_mla = DEPTH // 2
    G, E, F = N_GROUPS, EXPERTS_PER_GROUP, EXPERT_FF

    def nrm(shape, scale):
        return jax.random.normal(next(ks), shape, f32) * scale

    def gain(shape):
        return 1.0 + 0.02 * jax.random.normal(next(ks), shape, f32)

    x = nrm((BATCH, SEQ, D), 1.0)
    c = nrm((BATCH, D), 1.0)
    offset = jax.random.randint(next(ks), (BATCH, 1), 0, MAX_POS_OFFSET, dtype=jnp.int32)
    positions = (offset + jnp.arange(SEQ, dtype=jnp.int32)[None, :]).astype(jnp.int32)
    qk_mla = MLA_NOPE + MLA_ROPE
    return {
        "x": x,
        "c": c,
        "positions": positions,
        "ada_w": nrm((DEPTH, D, 6 * D), 0.5 * D ** -0.5),
        "ada_b": nrm((DEPTH, 6 * D), 0.02),
        "norm_mix": gain((DEPTH, D)),
        "norm_ffn": gain((DEPTH, D)),
        "da_w_qkv": nrm((n_da, D, 3 * D), D ** -0.5),
        "da_q_norm": gain((n_da, DA_HEAD_DIM)),
        "da_k_norm": gain((n_da, DA_HEAD_DIM)),
        "da_lambda_q1": nrm((n_da, DA_HEAD_DIM), 0.1),
        "da_lambda_k1": nrm((n_da, DA_HEAD_DIM), 0.1),
        "da_lambda_q2": nrm((n_da, DA_HEAD_DIM), 0.1),
        "da_lambda_k2": nrm((n_da, DA_HEAD_DIM), 0.1),
        "da_subln": gain((n_da, 2 * DA_HEAD_DIM)),
        "da_w_o": nrm((n_da, D, D), D ** -0.5),
        "mla_w_in": nrm((n_mla, D, MLA_Q_RANK + MLA_KV_RANK + MLA_ROPE), D ** -0.5),
        "mla_q_a_norm": gain((n_mla, MLA_Q_RANK)),
        "mla_kv_a_norm": gain((n_mla, MLA_KV_RANK)),
        "mla_w_uq": nrm((n_mla, MLA_Q_RANK, MLA_HEADS * qk_mla), MLA_Q_RANK ** -0.5),
        "mla_w_ukv": nrm((n_mla, MLA_KV_RANK, MLA_HEADS * (MLA_NOPE + MLA_V)), MLA_KV_RANK ** -0.5),
        "mla_q_nope_norm": gain((n_mla, MLA_NOPE)),
        "mla_q_pe_norm": gain((n_mla, MLA_ROPE)),
        "mla_k_nope_norm": gain((n_mla, MLA_NOPE)),
        "mla_k_pe_norm": gain((n_mla, MLA_ROPE)),
        "mla_w_o": nrm((n_mla, MLA_HEADS * MLA_V, D), (MLA_HEADS * MLA_V) ** -0.5),
        "moe_w_group": nrm((DEPTH, D, G), D ** -0.5),
        "moe_b_group": nrm((DEPTH, G), 0.01),
        "moe_w_router": nrm((DEPTH, D, G * E), D ** -0.5),
        "moe_b_router": nrm((DEPTH, G, E), 0.01),
        "moe_w1": nrm((DEPTH, G, E, D, F), D ** -0.5),
        "moe_w3": nrm((DEPTH, G, E, D, F), D ** -0.5),
        "moe_w2": nrm((DEPTH, G, E, F, D), F ** -0.5),
    }

def reference(x, c, positions, ada_w, ada_b, norm_mix, norm_ffn,
              da_w_qkv, da_q_norm, da_k_norm, da_lambda_q1, da_lambda_k1, da_lambda_q2, da_lambda_k2,
              da_subln, da_w_o,
              mla_w_in, mla_q_a_norm, mla_kv_a_norm, mla_w_uq, mla_w_ukv,
              mla_q_nope_norm, mla_q_pe_norm, mla_k_nope_norm, mla_k_pe_norm, mla_w_o,
              moe_w_group, moe_b_group, moe_w_router, moe_b_router, moe_w1, moe_w3, moe_w2):
    cos_da, sin_da = rope_tables(positions, DA_HEAD_DIM)
    cos_mla, sin_mla = rope_tables(positions, MLA_ROPE)
    cond = jax.nn.silu(c)
    for i in range(DEPTH):
        mod = cond @ ada_w[i] + ada_b[i]
        sh_m, sc_m, g_m, sh_f, sc_f, g_f = jnp.split(mod, 6, axis=-1)
        h = modulate(rms_norm(x, norm_mix[i]), sh_m, sc_m)
        j = i // N_MIXERS
        if i % N_MIXERS == 0:
            lambda_init = 0.8 - 0.6 * math.exp(-0.3 * i)
            y = diff_attention(h, cos_da, sin_da, da_w_qkv[j], da_q_norm[j], da_k_norm[j],
                               da_lambda_q1[j], da_lambda_k1[j], da_lambda_q2[j], da_lambda_k2[j],
                               da_subln[j], da_w_o[j], lambda_init)
        else:
            y = mla_attention(h, cos_mla, sin_mla, mla_w_in[j], mla_q_a_norm[j], mla_kv_a_norm[j],
                              mla_w_uq[j], mla_w_ukv[j], mla_q_nope_norm[j], mla_q_pe_norm[j],
                              mla_k_nope_norm[j], mla_k_pe_norm[j], mla_w_o[j])
        x = x + g_m[:, None, :] * y
        h = modulate(rms_norm(x, norm_ffn[i]), sh_f, sc_f)
        x = x + g_f[:, None, :] * hier_moe(h, moe_w_group[i], moe_b_group[i], moe_w_router[i],
                                           moe_b_router[i], moe_w1[i], moe_w3[i], moe_w2[i])
    return x


_drawn_inputs = setup_inputs


def setup_inputs(seed=0):
    import zlib

    import numpy as np

    out = dict(_drawn_inputs(seed))
    spreads = {}
    factors = {'norm_mix': 5.096,
     'norm_ffn': 3.09,
     'da_q_norm': 6.633,
     'da_k_norm': 6.328,
     'da_lambda_q1': 8.0,
     'da_subln': 5.057,
     'mla_q_a_norm': 8.0,
     'mla_kv_a_norm': 8.0,
     'mla_q_nope_norm': 8.0,
     'mla_q_pe_norm': 8.0,
     'mla_k_nope_norm': 8.0,
     'mla_k_pe_norm': 8.0,
     'moe_b_group': 5.582,
     'moe_b_router': 2.853}
    for name, (base, spread) in spreads.items():
        noise = np.random.default_rng([zlib.crc32(name.encode()), seed]).standard_normal(out[name].shape)
        drawn = base * np.exp(spread * noise) if base else spread * noise
        out[name] = __import__('jax').numpy.asarray(drawn.astype(out[name].dtype))
    for name, factor in factors.items():
        out[name] = (out[name] * factor).astype(out[name].dtype)
    return out
```

```python
import math
from contextlib import ExitStack

import concourse.bass as bass
from concourse import mybir

F32 = mybir.dt.float32
I32 = mybir.dt.int32
ALU = mybir.AluOpType
ACT = mybir.ActivationFunctionType
AX = mybir.AxisListType

P = 128
D = 1024
S = 512
T = S // P
C = D // P
EPS = 1e-6
NEG = -1e30

DH = 64
DA_H = 8
LAMBDA_INIT = 0.8 - 0.6 * math.exp(0.0)
NOPE, ROPE, VD = 64, 32, 64
QK = NOPE + ROPE
MLA_H = 16
QR, KVR = 384, 256
QRC, KVC = QR // P, KVR // P

G, EPG, E, FF = 4, 8, 32, 256
CAP = 64
PAIRS = E // 2
OVER = 2 * S // CAP - 1
TAILS = (OVER + 1) // 2
NPAIR = PAIRS + TAILS
NSLOT = NPAIR * P
NOWHERE = 1 << 20
NR = G + E

UNIT = 2048
AHEAD = 8
RING = 6
NH = 512

MAGIC = 1.5 * 2.0 ** 23
TWO_PI = 2 * math.pi
PI_A = 6.28125
PI_B = 0.0019350051879882812
PI_C = TWO_PI - PI_A - PI_B


class Chain:

    def __init__(self, eng, sem):
        self.eng, self.sem, self.n = eng, sem, 0

    def link(self, instruction):
        self.n += 1
        instruction.then_inc(self.sem, 1)
        self.eng.wait_ge(self.sem, self.n)


def wait(eng, sem, value):
    if isinstance(value, int) and value <= 0:
        return
    eng.wait_ge(sem, value)


def ada_after(n):
    before = AHEAD + sum(2 if m % 3 < 2 else 1 for m in range(n))
    return range(before, before + (2 if n % 3 < 2 else 1))


def ring_plan(A):
    ada = [A["ada_w"][l].rearrange("(p c) n -> p c n", c=C) for l in range(2)]
    qkv = A["da_w_qkv"][0].rearrange("(p c) n -> p c n", c=C)

    def ada_unit(u, slot):
        l, g, c = u // 24, u // 8 % 3, u % 8
        return ("ada", u), ada[l][:, c:c + 1, g * UNIT:(g + 1) * UNIT], 1, slot, ("ada", u + 1)

    def qkv_units(x):
        n = (x % 3) * D + (x // 3) * NH
        return [(("qkv", x, half), qkv[:, 4 * half:4 * half + 4, n:n + NH], 4, 2 * ((x + 1) % 2) + half,
                 ("da_mm", 4 * x + 4)) for half in range(2)]

    first = [ada_unit(u, u % RING) for u in range(AHEAD)] + qkv_units(0)
    for n in range(24):
        if n % 4 == 1 and n < 20:
            first += qkv_units(n // 4 + 1)
        first += [ada_unit(u, 4 + u % 2) for u in ada_after(n)]
    wo = A["da_w_o"][0].rearrange("(k p) n -> p k n", p=P)
    first += [(("wo", u), wo[:, 2 * u:2 * u + 2, :], 2, 2 + u, ("wo", 2 * T)) for u in range(4)]
    w_in = A["mla_w_in"][0].rearrange("(p c) n -> p c n", c=C)
    second = [(("in", c0 // 3), w_in[:, c0:c1, :], c1 - c0, ("lat", 2 * T)) for c0, c1 in ((0, 3), (3, 6), (6, 8))]
    uq = A["mla_w_uq"][0].rearrange("(k p) n -> p k n", p=P)
    second += [(("uq", k), uq[:, k:k + 1, :], 1, ("mla_kv", 4 * T)) for k in range(QRC)]
    ukv = A["mla_w_ukv"][0].rearrange("(k p) n -> p k n", p=P)
    second += [(("ukv", k), ukv[:, k:k + 1, :], 1, ("mla_kv", 4 * T)) for k in range(KVC)]
    wo = A["mla_w_o"][0].rearrange("(k p) n -> p k n", p=P)
    second += [(("wo", u), wo[:, 2 * u:2 * u + 2, :], 2, ("wo", 4 * T)) for u in range(4)]
    return first, [(key, src, k, n % RING, free) for n, (key, src, k, free) in enumerate(second)]


def build(nc, A, inv_da, inv_mla, out):
    stack = ExitStack()
    with stack:
        enter = stack.enter_context

        def sb(name, shape, dt=F32):
            return enter(nc.sbuf_tensor(name, shape, dt))

        sems = {}

        def sem(name):
            if name not in sems:
                sems[name] = enter(nc.semaphore("s_" + name))
            return sems[name]

        mod_d = nc.dram_tensor("mod_d", [2, 6 * D], F32)
        xn_d = [nc.dram_tensor(f"xn_d{l}", [S, D], F32) for l in range(2)]
        y_d = [nc.dram_tensor(f"y_d{l}", [2 * S, D], F32) for l in range(2)]
        tab_d = [nc.dram_tensor(f"tab_d{l}", [NSLOT, 1], I32) for l in range(2)]

        ring = sb("ring", [P, RING, UNIT])
        X = sb("X", [P, T, D])
        RA = sb("RA", [P, 4096])
        RH = sb("RH", [P, 4096])
        RV = sb("RV", [P, 4096])
        RQK = sb("RQK", [P, RING * UNIT])
        SCR = sb("SCR", [P, 4096])
        PS = sb("PS", [P, 3072])
        GM = sb("GM", [P, D])
        GF = sb("GF", [P, D])
        MR = sb("MR", [P, NH])
        ident = sb("ident", [P, P])
        tri = sb("tri", [P, P])
        ones = sb("ones", [P, P])
        mneg = sb("mneg", [P, P])
        WGR = sb("WGR", [P, C, NR])
        RT = sb("RT", [P, T, 4, ROPE])
        small = sb("small", [P, 1088])
        idx = sb("idx", [P, 2, NPAIR], I32)
        ci = sb("ci", [P, 4], I32)
        pid = sb("pid", [P, T, 2], I32)
        sloti = sb("sloti", [P, T, 2], I32)
        CTL = sb("CTL", [1, 1 + 2 * TAILS], I32)
        posi = sb("posi", [P, T], I32)

        bump = [0]

        def sm(*shape):
            n = math.prod(shape)
            v = small[:, bump[0]:bump[0] + n]
            bump[0] += n
            assert bump[0] <= 1088
            if len(shape) == 2:
                return v.rearrange("p (a b) -> p a b", a=shape[0])
            if len(shape) == 3:
                return v.rearrange("p (a b c) -> p a b c", a=shape[0], b=shape[1])
            return v

        MODC = sm(2, 4, C)
        NRM = sm(2, 2, C)
        GC = sm(4, C)
        cc = sm(C)
        condr = sm(C, 32)
        eps = sm(1)
        ss = sm(8)
        sd = sm(8)
        rs = sm(8)
        hss = sm(2, 32)
        hsd = sm(2, 32)
        hrs = sm(2, 32)
        mx, nmx, ls, rl = sm(2, 2), sm(2, 2), sm(2, 2), sm(2, 2)
        lamv = sm(4, DH)
        lam = sm(4)
        subc = sm(1)
        qnc, knc = sm(1), sm(1)
        qan, kvan = sm(QRC), sm(KVC)
        posf = sm(T)
        invs = sm(DH // 2 + ROPE // 2)
        Wt = sm(T, 2)
        th = sm(7)
        i8 = sm(EPG)
        i32f = sm(E)
        i16f = sm(2 * TAILS)
        bgr = sm(NR)
        gnb = RV[:, 1024:1024 + 2 * DH + 2 * ROPE]

        def view(region, at, *shape):
            v = region[:, at:at + math.prod(shape)]
            if len(shape) == 2:
                return v.rearrange("p (a b) -> p a b", a=shape[0])
            if len(shape) == 3:
                return v.rearrange("p (a b c) -> p a b c", a=shape[0], b=shape[1])
            if len(shape) == 4:
                return v.rearrange("p (a b c d) -> p a b c d", a=shape[0], b=shape[1], c=shape[2])
            return v

        XN = view(RA, 0, T, D)
        HT = view(RH, 0, C, S)
        OTOK = view(RH, 0, T, D)
        OT = view(RA, 0, C, S)
        V = view(RV, 0, T, D)
        daq = view(RQK, 0, DA_H, S)
        dak = [view(RQK, 4096 * (1 + c), DA_H, S) for c in range(2)]
        mq = [view(RQK, 2048 * b, 4, S) for b in range(2)]
        mk = [view(RQK, 4096 + 2048 * b, 4, S) for b in range(2)]
        CT = view(RA, 0, QRC + KVC, S)
        pr = [view(SCR, 1024 * b, 2, S) for b in range(2)]
        aT = [view(SCR, 2048 + 1024 * b, 2, S) for b in range(2)]
        DT = view(SCR, 0, T, 4, DH)
        SQ, M1, M2, YT = (view(PS, NH * n, NH) for n in range(4))
        LT_ = view(PS, 0, QR + KVR)
        KP = view(PS, 2560, T, ROPE)
        QY, KY = view(PS, 1024, 4, QK), view(PS, 1024 + 4 * QK, 4, QK)
        xg = [view(RV, 1024 * b, D) for b in range(2)]
        xgT = [view(RV, 2048 + 1024 * b, C, P) for b in range(2)]
        ysb = [view(PS, 1024 * b, D) for b in range(2)]
        sil = view(PS, 2048, FF)
        hid = view(PS, 2048 + FF, 2, P)
        hidT = view(PS, 2048 + 2 * FF, 2, P)
        YP = [view(RH, 0, 2, D), view(RH, 2048, 2, D), view(RA, 0, 2, D), view(RA, 2048, 2, D)]
        bank = [ring, RQK[:, :].rearrange("p (s n) -> p s n", s=RING)]

        PB = [enter(nc.psum_tensor(f"PB{n}", [P, NH], F32)) for n in range(8)]

        streams = ring_plan(A)
        plan, arrival, fills, holder = [], [{}, {}], [0] * (2 * RING), [None] * RING
        first_slot, moe_fills, moe_holder = [], [], []
        for l in range(2):
            now = []
            for key, src, k, slot, free in streams[l]:
                fills[slot] += 1
                now.append((src, k, slot, holder[slot]))
                arrival[l][key] = (slot, 16 * fills[slot])
                holder[slot] = free
            plan.append(now)
            first_slot.append((slot + 1) % RING)
            moe_fills.append(list(fills))
            moe_holder.append(list(holder))
            for s in range(2 * RING):
                fills[s] += PAIRS // 2
            holder = [(f"y{l}", PAIRS - 1)] * RING
        s_w = [sem(f"w{s}") for s in range(2 * RING)]

        w1 = [A["moe_w1"][l].rearrange("g e (p c) f -> (g e) p (c f)", c=C) for l in range(2)]
        w3 = [A["moe_w3"][l].rearrange("g e (p c) f -> (g e) p (c f)", c=C) for l in range(2)]
        w2 = [A["moe_w2"][l].rearrange("g e (p c) d -> (g e) p (c d)", c=FF // P) for l in range(2)]

        def slots(l):
            return [(first_slot[l] + k) % RING for k in range(6)]

        block = enter(nc.Block())

        @block.sync
        def _(sp):
            def stream(l):
                for src, k, slot, held in plan[l]:
                    if held:
                        sp.wait_ge(sem(held[0]), held[1])
                    cols = src.shape[-1]
                    dst = ring[:, slot, 0:k * cols].rearrange("p (k n) -> p k n", k=k)
                    sp.dma_start(dst, src).then_inc(s_w[slot], 16)

            def experts(l, b, free, e0, e1, arrive):
                for k, (w, e) in enumerate(((w1, e0), (w1, e1), (w3, e0), (w3, e1), (w2, e0), (w2, e1))):
                    free(k)
                    src = w[l][bass.ds(e, 1)].rearrange("a p n -> p (a n)")
                    sp.dma_start(bank[b][:, slots(l)[k], :], src).then_inc(arrive(k), 16)

            def main(l, i, b):
                def free(k):
                    if isinstance(i, int) and i == 0:
                        if b == 0:
                            name, value = moe_holder[l][slots(l)[k]]
                            sp.wait_ge(sem(name), value)
                        if b == 1:
                            sp.wait_ge(sem("sc"), 32 * (l + 1))
                    else:
                        sp.wait_ge(sem(f"{'aby'[k // 2]}{l}"), 2 * i + b - 1)
                experts(l, b, free, 4 * i + 2 * b, 4 * i + 2 * b + 1,
                        lambda k: s_w[RING * b + slots(l)[k]])

            for l in range(2):
                stream(l)
                for b in range(2):
                    main(l, 0, b)
                with sp.Fori(1, PAIRS // 2) as i:
                    for b in range(2):
                        main(l, i, b)
                sp.wait_ge(sem("ctl"), l + 1)
                tails = sp.value_load(CTL[0:1, 0:1], min_val=0, max_val=TAILS)
                with sp.Fori(0, TAILS) as j:
                    with sp.If(j < tails):
                        e0 = sp.value_load(CTL[0:1, bass.ds(2 * j + 1, 1)], min_val=0, max_val=E - 1)
                        e1 = sp.value_load(CTL[0:1, bass.ds(2 * j + 2, 1)], min_val=0, max_val=E - 1)
                        experts(l, 1, lambda k: sp.wait_ge(sem(f"y{l}"), PAIRS + j) if k == 0 else None,
                                e0, e1, lambda k: sem(f"wt{l}"))
            for t in range(T):
                sp.wait_ge(sem("comb"), T + t + 1)
                sp.dma_start(out[t * P:(t + 1) * P, :], X[:, t, :]).then_inc(sem("out"), 16)
            sp.wait_ge(sem("out"), 16 * T)

        @block.tensor
        def _(pe):
            mm = nc.tensor.matmul

            def take(l, *key):
                slot, value = arrival[l][key]
                pe.wait_ge(s_w[slot], value)
                return ring[:, slot, :]

            def ada(u):
                w = take(0, "ada", u)
                a, c = divmod(u, C)
                if c == 0:
                    wait(pe, sem("mr"), a - 1)
                for j in range(4):
                    last = mm(PB[5 + a % 2][32 * j:32 * j + 32, :], condr[:, c, :], w[:, j * NH:(j + 1) * NH],
                              start=c == 0, stop=c == C - 1)
                last.then_inc(sem("ada"), 1)

            def transpose_x(k):
                if k in (1, 3):
                    pe.wait_ge(sem("oev"), 8 * (k // 2 + 1))
                for t in range(T):
                    pe.wait_ge(sem("xn"), 4 * k + t + 1)
                    for c in range(C):
                        last = nc.tensor.transpose(PB[c][:, t * P:(t + 1) * P], XN[:, t, c * P:(c + 1) * P], ident[:, :])
                    last.then_inc(sem("xt"), 1)

            def da_project():
                def turn(n):
                    m = (n // 12) * 8 + n % 12
                    wait(pe, sem("datev"), m)
                    pe.wait_ge(sem("day"), m + 1)
                    for h in range(4):
                        last = nc.tensor.transpose(PB[4][:, h * P:(h + 1) * P], YT[:, h * P:(h + 1) * P], ident[:, :])
                    last.then_inc(sem("dat"), 1)

                for hb in range(2):
                    for w in range(3):
                        us = [take(0, "qkv", 3 * hb + w, half) for half in range(2)]
                        for t in range(T):
                            n = hb * 12 + w * 4 + t
                            wait(pe, sem("daev"), n - 3)
                            for c in range(C):
                                last = mm(PB[n % 4][:, :], HT[:, c, t * P:(t + 1) * P],
                                          us[c // 4][:, (c % 4) * NH:(c % 4 + 1) * NH], start=c == 0, stop=c == C - 1)
                            last.then_inc(sem("da_mm"), 1)
                            if 0 < n and (n - 1) % 12 < 8:
                                turn(n - 1)
                            for u in ada_after(n):
                                ada(u)

            def attention(l, i0, i1):
                def scores(i):
                    g, t = divmod(i, T)
                    n = 32 * l + i
                    wait(pe, sem("exp"), n - 1)
                    L = (t + 1) * P
                    for a in range(2):
                        o = PB[2 * (i % 2) + a]
                        if l == 0:
                            mm(o[:, 0:L], daq[:, g, t * P:L], dak[a][:, g, 0:L], start=True, stop=False)
                        else:
                            h = 2 * (g % 2) + a
                            mm(o[:, 0:L], mq[g // 2 % 2][0:QK, h, t * P:L], mk[g // 2 % 2][0:QK, h, 0:L],
                               start=True, stop=False)
                        last = mm(o[:, t * P:L], ident[:, :], mneg[:, :], start=False, stop=True)
                    last.then_inc(sem("sc"), 1)

                def turn(i):
                    t, b, n = i % T, i % 2, 32 * l + i
                    pe.wait_ge(sem("exp" if l else "p"), n + 1)
                    wait(pe, sem("tev"), n)
                    if l == 1:
                        wait(pe, sem("tev1"), i)
                    for a in range(1 + l):
                        for k in range(t + 1):
                            last = nc.tensor.transpose(PB[4 + a][:, k * P:(k + 1) * P], pr[b][:, a, k * P:(k + 1) * P], ident[:, :])
                    last.then_inc(sem("tr"), 1)

                def values(i):
                    (g, t), b, n = divmod(i, T), i % 2, 32 * l + i
                    pe.wait_ge(sem("tev"), n + 1)
                    if l == 1:
                        pe.wait_ge(sem("tev1"), i + 1)
                    wait(pe, sem("oe"), n - 1)
                    if l == 0:
                        for k in range(t + 1):
                            last = mm(PB[6 + b][:, 0:P], aT[b][:, 0, k * P:(k + 1) * P], V[:, k, g * P:(g + 1) * P],
                                      start=k == 0, stop=k == t)
                    else:
                        for a in range(2):
                            h = 2 * g + a
                            for k in range(t + 1):
                                last = mm(PB[6 + b][:, a * VD:(a + 1) * VD], aT[b][:, a, k * P:(k + 1) * P],
                                          V[:, k, h * VD:(h + 1) * VD], start=k == 0, stop=k == t)
                    last.then_inc(sem("av"), 1)

                scores(i0)
                scores(i0 + 1)
                for i in range(i0, i1):
                    if i + 2 < i1:
                        scores(i + 2)
                    turn(i)
                    if i > i0:
                        values(i - 1)
                values(i1 - 1)

            def project_out(l):
                for t in range(T):
                    if l == 0:
                        pe.wait_ge(sem("on"), t + 1)
                    else:
                        pe.wait_ge(sem("oe"), 64)
                    for half in range(2):
                        m = 8 * l + 2 * t + half
                        wait(pe, sem("otev"), m - 1)
                        for k in range(4):
                            h = 4 * half + k
                            last = nc.tensor.transpose(PB[4 + half][:, k * P:(k + 1) * P], OTOK[:, t, h * P:(h + 1) * P], ident[:, :])
                        last.then_inc(sem("ott"), 1)
                us = [take(l, "wo", u) for u in range(4)]
                pe.wait_ge(sem("otev"), 8 * (l + 1))
                for t in range(T):
                    for n in range(2):
                        m = 2 * t + n
                        for k in range(C):
                            last = mm(PB[m][:, :], OT[:, k, t * P:(t + 1) * P],
                                      us[k // 2][:, (k % 2) * D + n * NH:(k % 2) * D + (n + 1) * NH],
                                      start=k == 0, stop=k == C - 1)
                        last.then_inc(sem("wo"), 1)

            def route(l):
                pe.wait_ge(sem("hA"), 4 * (2 * l + 2))
                pe.wait_ge(sem("hD"), 4 * (2 * l + 2))
                pe.wait_ge(sem("wgr"), 32 * (l + 1))
                for t in range(T):
                    for c in range(C):
                        last = mm(PB[0][:, t * NR:(t + 1) * NR], HT[:, c, t * P:(t + 1) * P], WGR[:, c, :],
                                  start=c == 0, stop=c == C - 1)
                last.then_inc(sem("lg"), 1)
                pe.wait_ge(sem("M"), l + 1)
                M = view(SCR, 256, T, E)
                for t in range(T):
                    for k in range(t + 1):
                        mm(PB[1][:, t * E:(t + 1) * E], (tri if k == t else ones)[:, :], M[:, k, :], start=k == 0, stop=k == t)
                for k in range(T):
                    last = mm(PB[1][:, T * E:(T + 1) * E], ones[:, :], M[:, k, :], start=k == 0, stop=k == T - 1)
                last.then_inc(sem("rank"), 1)

            def expert_step(l, b, q, n, wb, arrived):
                pe.wait_ge(sem(f"gath{l}{b}"), 16 * (q + 1))
                wait(pe, sem(f"xA{l}"), n)
                wait(pe, sem(f"xD{l}"), n)
                for c in range(C):
                    last = nc.tensor.transpose(PB[c % 2][:, (c // 2) * P:(c // 2 + 1) * P], xg[b][:, c * P:(c + 1) * P], ident[:, :])
                last.then_inc(sem(f"xt{l}"), 1)
                arrived(0)
                pe.wait_ge(sem(f"xA{l}"), n + 1)
                pe.wait_ge(sem(f"xD{l}"), n + 1)
                for m, (o, done, read) in enumerate(((PB[2], "a", "sil"), (PB[3], "b", "hid"))):
                    if m:
                        arrived(1)
                    wait(pe, sem(f"{read}{l}"), n)
                    for c in range(C):
                        for e in range(2):
                            last = mm(o[CAP * e:CAP * (e + 1), 0:FF], xgT[b][:, c, CAP * e:CAP * (e + 1)],
                                      bank[wb][:, slots(l)[2 * m + e], c * FF:(c + 1) * FF], start=c == 0, stop=c == C - 1)
                    last.then_inc(sem(f"{done}{l}"), 1)
                pe.wait_ge(sem(f"hid{l}"), n + 1)
                wait(pe, sem(f"hT{l}"), n)
                for c in range(2):
                    last = nc.tensor.transpose(PB[4][:, c * P:(c + 1) * P], hid[:, c, :], ident[:, :])
                last.then_inc(sem(f"ht{l}"), 1)
                arrived(2)
                pe.wait_ge(sem(f"hT{l}"), n + 1)
                wait(pe, sem(f"yA{l}"), n)
                wait(pe, sem(f"yD{l}"), n)
                for m in range(2):
                    for c in range(2):
                        for e in range(2):
                            last = mm(PB[5 + m][CAP * e:CAP * (e + 1), :], hidT[:, c, CAP * e:CAP * (e + 1)],
                                      bank[wb][:, slots(l)[4 + e], c * D + m * NH:c * D + (m + 1) * NH], start=c == 0, stop=c == 1)
                last.then_inc(sem(f"y{l}"), 1)

            def experts(l):
                def step(i, b):
                    def arrived(m):
                        for e in range(2):
                            s = RING * b + slots(l)[2 * m + e]
                            pe.wait_ge(s_w[s], 16 * (moe_fills[l][s] + 1) + 16 * i)
                    expert_step(l, b, i, 2 * i + b, b, arrived)
                for b in range(2):
                    step(0, b)
                with pe.Fori(1, PAIRS // 2) as i:
                    for b in range(2):
                        step(i, b)
                pe.wait_ge(sem("ctl"), l + 1)
                tails = pe.value_load(CTL[0:1, 0:1], min_val=0, max_val=TAILS)
                with pe.Fori(0, TAILS) as j:
                    with pe.If(j < tails):
                        pe.wait_ge(sem(f"wt{l}"), 96 * j + 96)
                        expert_step(l, 0, PAIRS // 2 + j, PAIRS + j, 1, lambda m: None)

            def latents():
                us = [take(1, "in", u) for u in range(3)]
                W = QR + KVR + ROPE

                def turn(t):
                    pe.wait_ge(sem("ln"), t + 1)
                    wait(pe, sem("ltevA"), t)
                    wait(pe, sem("ltevD"), t)
                    for k in range(QRC + KVC):
                        o = PB[4][:, k * P:(k + 1) * P] if k < QRC else PB[5][:, (k - QRC) * P:(k - QRC + 1) * P]
                        last = nc.tensor.transpose(o, LT_[:, k * P:(k + 1) * P], ident[:, :])
                    last.then_inc(sem("ltt"), 1)

                for t in range(T):
                    wait(pe, sem("lev"), t - 1)
                    for m, (c0, c1) in enumerate(((0, QR), (QR, W))):
                        for c in range(C):
                            last = mm(PB[2 * (t % 2) + m][:, 0:c1 - c0], HT[:, c, t * P:(t + 1) * P],
                                      us[c // 3][:, (c % 3) * W + c0:(c % 3) * W + c1], start=c == 0, stop=c == C - 1)
                        last.then_inc(sem("lat"), 1)
                    if t:
                        turn(t - 1)
                turn(T - 1)

            def mla():
                uq = [take(1, "uq", k) for k in range(QRC)]
                ukv = [take(1, "ukv", k) for k in range(KVC)]

                def turn(n):
                    pe.wait_ge(sem("my"), n + 1)
                    wait(pe, sem("mtev"), n)
                    wait(pe, sem("mtevD"), n)
                    for m, y in enumerate((QY, KY)):
                        for h in range(4):
                            last = nc.tensor.transpose(PB[4 + m][0:QK, h * P:(h + 1) * P], y[:, h, :], ident[:, :])
                    last.then_inc(sem("mt"), 1)

                pe.wait_ge(sem("ltevA"), T)
                pe.wait_ge(sem("ltevD"), T)
                for hb in range(4):
                    if hb:
                        pe.wait_ge(sem("exp"), 32 + 8 * hb)
                        pe.wait_ge(sem("tev"), 32 + 8 * hb)
                        pe.wait_ge(sem("tev1"), 8 * hb)
                    for t in range(T):
                        n = hb * T + t
                        wait(pe, sem("mev"), n - 1)
                        wait(pe, sem("mvev"), n - 1)
                        for k in range(QRC):
                            last = mm(PB[n % 2][:, 0:4 * QK], CT[:, k, t * P:(t + 1) * P],
                                      uq[k][:, hb * 4 * QK:(hb + 1) * 4 * QK], start=k == 0, stop=k == QRC - 1)
                        last.then_inc(sem("mla_q"), 1)
                        for k in range(KVC):
                            last = mm(PB[2 + n % 2][:, :], CT[:, QRC + k, t * P:(t + 1) * P],
                                      ukv[k][:, hb * NH:(hb + 1) * NH], start=k == 0, stop=k == KVC - 1)
                        last.then_inc(sem("mla_kv"), 1)
                        if t:
                            turn(n - 1)
                    turn(hb * T + T - 1)
                    pe.wait_ge(sem("mtev"), 4 * hb + 4)
                    pe.wait_ge(sem("mtevD"), 4 * hb + 4)
                    pe.wait_ge(sem("mvev"), 4 * hb + 4)
                    pe.wait_ge(sem("mev"), 4 * hb + 4)
                    attention(1, 8 * hb, 8 * hb + 8)

            pe.wait_ge(sem("const"), 3)
            pe.wait_ge(sem("cond"), 1)
            for u in range(AHEAD):
                ada(u)
            pe.wait_ge(sem("mr"), 1)
            transpose_x(0)
            pe.wait_ge(sem("hA"), 4)
            pe.wait_ge(sem("hD"), 4)
            da_project()
            pe.wait_ge(sem("mr"), 6)
            pe.wait_ge(sem("datev"), 16)
            pe.wait_ge(sem("daev"), 24)
            pe.wait_ge(sem("pool"), 5)
            attention(0, 0, 32)
            project_out(0)
            transpose_x(1)
            route(0)
            experts(0)
            transpose_x(2)
            pe.wait_ge(sem("hA"), 12)
            pe.wait_ge(sem("hD"), 12)
            latents()
            mla()
            project_out(1)
            transpose_x(3)
            route(1)
            experts(1)

        @block.scalar
        def _(act):
            fn = nc.scalar.activation
            chain = Chain(act, sem("act"))

            def bc(v, n=P):
                return v.partition_broadcast(n)

            loads = [
                (cc, A["c"][0].rearrange("(p c) -> p c", c=C)),
                (posi[:, :], A["positions"][0].rearrange("(t p) -> p t", p=P)),
                (NRM[:, 0], A["norm_mix"].rearrange("l (p c) -> p l c", c=C)),
                (NRM[:, 1], A["norm_ffn"].rearrange("l (p c) -> p l c", c=C)),
                (gnb[:, 0:DH], bc(A["da_q_norm"][0])),
                (gnb[:, DH:2 * DH], bc(A["da_k_norm"][0])),
                (gnb[:, 2 * DH:2 * DH + ROPE], bc(A["mla_q_pe_norm"][0])),
                (gnb[:, 2 * DH + ROPE:], bc(A["mla_k_pe_norm"][0])),
                (lamv[:, 0], bc(A["da_lambda_q1"][0])),
                (lamv[:, 1], bc(A["da_lambda_k1"][0])),
                (lamv[:, 2], bc(A["da_lambda_q2"][0])),
                (lamv[:, 3], bc(A["da_lambda_k2"][0])),
                (subc, A["da_subln"][0].rearrange("(p c) -> p c", c=1)),
                (qnc[0:NOPE, :], A["mla_q_nope_norm"][0].rearrange("(p c) -> p c", c=1)),
                (knc[0:NOPE, :], A["mla_k_nope_norm"][0].rearrange("(p c) -> p c", c=1)),
                (qan, A["mla_q_a_norm"][0].rearrange("(k p) -> p k", p=P)),
                (kvan, A["mla_kv_a_norm"][0].rearrange("(k p) -> p k", p=P)),
                (invs[:, 0:DH // 2], bc(inv_da)),
                (invs[:, DH // 2:], bc(inv_mla)),
            ]
            for dst, src in loads:
                with nc.allow_non_contiguous_dma(reason="short vectors"):
                    act.dma_start(dst, src).then_inc(sem("in"), 16)
            assert len(loads) == N_IN
            for t in range(T):
                act.dma_start(X[:, t, :], A["x"][0, t * P:(t + 1) * P, :]).then_inc(sem("x"), 16)

            act.wait_ge(sem("in"), 16 * N_IN)
            fn(cc, cc, ACT.Silu).then_inc(sem("silc"), 1)
            act.wait_ge(sem("lams"), 1)
            fn(lam[:, 0:2], lam[:, 0:2], ACT.Exp).then_inc(sem("lame"), 1)
            act.wait_ge(sem("ang"), 1)
            fn(view(RH, 2048, T, 48), view(RH, 0, T, 48), ACT.Sin)
            fn(view(RH, 2560, T, 48), view(RH, 0, T, 48), ACT.Sin, scale=0.5).then_inc(sem("sin"), 1)

            def norm(k):
                for t in range(T):
                    if k == 0:
                        act.wait_ge(sem("x"), 16 * T)
                    elif k == 2:
                        act.wait_ge(sem("comb"), t + 1)
                    else:
                        act.wait_ge(sem("res"), 4 * (k // 2) + t + 1)
                    if t == 0:
                        wait(act, sem("xn"), 4 * k)
                    wait(act, sem("sd"), 4 * k + t)
                    fn(view(PS, 0, D), X[:, t, :], ACT.Square, accum_out=ss[:, t:t + 1]).then_inc(sem("sq"), 1)
                    act.wait_ge(sem("sq"), 4 * k + t + 1)
                    fn(sd[:, t:t + 1], ss[:, t:t + 1], ACT.Sqrt, bias=eps, scale=1.0 / D).then_inc(sem("sd"), 1)

            def modulate(k):
                l, w = divmod(k, 2)
                act.wait_ge(sem("gc"), k + 1)
                act.wait_ge(sem("xt"), 4 * k + 4)
                for c in range(0, C, 2):
                    fn(HT[:, c, :], PB[c][:, :], ACT.Identity, bias=MODC[:, l, 2 * w, c:c + 1],
                       scale=GC[:, k, c:c + 1]).then_inc(sem("hA"), 1)

            def root(out_, in_, scale, s):
                fn(out_, in_, ACT.Sqrt, bias=eps, scale=scale).then_inc(sem(s), 1)

            def da_project():
                def turned(m):
                    n = (m // 8) * 12 + m % 8
                    hb, w, t = n // 12, n % 12 // 4, n % 4
                    act.wait_ge(sem("dat"), m + 1)
                    src = PB[4][:, :].rearrange("p (h q) -> p h q", h=4)
                    if w == 0:
                        fn(daq[:, 4 * hb:4 * hb + 4, t * P:(t + 1) * P], src, ACT.Identity).then_inc(sem("datev"), 1)
                    else:
                        for a in range(2):
                            last = fn(dak[a][64 * a:64 * a + 64, 4 * hb:4 * hb + 4, t * P:(t + 1) * P],
                                      src[64 * a:64 * a + 64], ACT.Identity)
                        last.then_inc(sem("datev"), 1)

                for hb in range(2):
                    for w in range(3):
                        for t in range(T):
                            n = hb * 12 + w * 4 + t
                            m = hb * 8 + w * 4 + t
                            act.wait_ge(sem("da_mm"), n + 1)
                            if w == 2:
                                act.wait_ge(sem("daev"), n)
                                fn(V[:, t, hb * NH:(hb + 1) * NH], PB[n % 4][:, :], ACT.Identity).then_inc(sem("daev"), 1)
                            else:
                                wait(act, sem("dss"), m)
                                fn(SQ, PB[n % 4][:, :], ACT.Square).then_inc(sem("dsq"), 1)
                                act.wait_ge(sem("dss"), m + 1)
                                wait(act, sem("drs"), m - 1)
                                root(hsd[:, m % 2, 0:8], hss[:, m % 2, 0:8], 1.0 / DH, "dsd")
                            if 0 < n and (n - 1) % 12 < 8:
                                turned((n - 1) // 12 * 8 + (n - 1) % 12)

            def attention(l, i0, i1):
                scale = DH ** -0.5 if l == 0 else QK ** -0.5

                def exps(i):
                    t, b, n = i % T, i % 2, 32 * l + i
                    L = (t + 1) * P
                    act.wait_ge(sem("nm"), n + 1)
                    wait(act, sem("tr"), n - 1)
                    wait(act, sem("p"), n - 1)
                    for a in range(2):
                        last = fn(pr[b][:, a, 0:L], PB[2 * b + a][:, 0:L], ACT.Exp, bias=nmx[:, b, a:a + 1],
                                  scale=scale, accum_out=ls[:, b, a:a + 1])
                    last.then_inc(sem("exp"), 1)

                def turned(i):
                    t, b, n = i % T, i % 2, 32 * l + i
                    L = (t + 1) * P
                    act.wait_ge(sem("tr"), n + 1)
                    wait(act, sem("av"), n - 1)
                    fn(aT[b][:, 0, 0:L], PB[4][:, 0:L], ACT.Identity).then_inc(sem("tev"), 1)

                def output(i):
                    (g, t), b, n = divmod(i, T), i % 2, 32 * l + i
                    act.wait_ge(sem("av"), n + 1)
                    fn(OTOK[:, t, g * P:(g + 1) * P], PB[6 + b][:, 0:P], ACT.Identity).then_inc(sem("oe"), 1)

                exps(i0)
                exps(i0 + 1)
                for i in range(i0, i1):
                    turned(i)
                    if i + 2 < i1:
                        exps(i + 2)
                    if l == 0 and i > i0:
                        output(i - 1)
                if l == 0:
                    output(i1 - 1)

            def output_norm():
                for t in range(T):
                    wait(act, sem("oss"), t)
                    if t == 0:
                        act.wait_ge(sem("oe"), 32)
                        act.wait_ge(sem("day"), 16)
                    fn(view(PS, 0, D), OTOK[:, t, :], ACT.Square).then_inc(sem("osq"), 1)
                    act.wait_ge(sem("oss"), t + 1)
                    root(hsd[:, 0, 8 * t:8 * t + 8], hss[:, 0, 8 * t:8 * t + 8], 1.0 / P, "osd")

            def output_turn(l):
                for t in range(T):
                    m = 8 * l + 2 * t
                    for half in range(2):
                        act.wait_ge(sem("ott"), m + half + 1)
                        dst = OT[:, 4 * half:4 * half + 4, t * P:(t + 1) * P]
                        src = PB[4 + half][:, :].rearrange("p (k q) -> p k q", k=4)
                        if l == 0:
                            fn(dst, src, ACT.Identity, scale=subc).then_inc(sem("otev"), 1)
                        else:
                            fn(dst, src, ACT.Identity).then_inc(sem("otev"), 1)

            def latents():
                for t in range(T):
                    o = [PB[2 * (t % 2)], PB[2 * (t % 2) + 1]]
                    act.wait_ge(sem("lat"), 2 * t + 2)
                    wait(act, sem("lrs"), t)
                    sq = view(PS, 1024, QR)
                    chain.link(fn(sq, o[0][:, 0:QR], ACT.Square, accum_out=ss[:, 4:5]))
                    chain.link(fn(sq[:, 0:KVR], o[1][:, 0:KVR], ACT.Square, accum_out=ss[:, 5:6]))
                    chain.link(fn(sq[:, 0:ROPE], o[1][:, KVR:KVR + ROPE], ACT.Square, accum_out=ss[:, 6:7]))
                    fn(sd[:, 4:5], ss[:, 4:5], ACT.Sqrt, bias=eps, scale=1.0 / QR)
                    fn(sd[:, 5:6], ss[:, 5:6], ACT.Sqrt, bias=eps, scale=1.0 / KVR)
                    fn(sd[:, 6:7], ss[:, 6:7], ACT.Sqrt, bias=eps, scale=1.0 / ROPE).then_inc(sem("lsd"), 1)
                    if t:
                        turn_latents(t - 1)
                turn_latents(T - 1)

            def turn_latents(t):
                act.wait_ge(sem("ltt"), t + 1)
                for k in range(QRC):
                    last = fn(CT[:, k, t * P:(t + 1) * P], PB[4][:, k * P:(k + 1) * P], ACT.Identity, scale=qan[:, k:k + 1])
                last.then_inc(sem("ltevA"), 1)

            def mla():
                def turned(n):
                    hb, t = divmod(n, T)
                    act.wait_ge(sem("mt"), n + 1)
                    wait(act, sem("sc"), 32 + 8 * (hb - 1))
                    fn(mq[hb % 2][0:QK, :, t * P:(t + 1) * P], PB[4][0:QK, :].rearrange("p (h q) -> p h q", h=4),
                       ACT.Identity, scale=qnc[0:QK, :]).then_inc(sem("mtev"), 1)

                for hb in range(4):
                    for t in range(T):
                        n = hb * T + t
                        act.wait_ge(sem("mla_q"), n + 1)
                        wait(act, sem("mss"), n)
                        sq = view(PS, 0, 4, QK)
                        sk = view(PS, 4 * QK, 4, NOPE)
                        kv = PB[2 + n % 2][:, :].rearrange("p (h x) -> p h x", h=4)
                        fn(sq, PB[n % 2][:, 0:4 * QK].rearrange("p (h x) -> p h x", h=4), ACT.Square)
                        act.wait_ge(sem("mla_kv"), n + 1)
                        fn(sk, kv[:, :, 0:NOPE], ACT.Square).then_inc(sem("msq"), 1)
                        act.wait_ge(sem("mss"), n + 1)
                        wait(act, sem("mrs"), n)
                        fn(hsd[:, 0, 0:8], hss[:, 0, 0:8], ACT.Sqrt, bias=eps, scale=1.0 / NOPE)
                        fn(hsd[:, 0, 8:12], hss[:, 0, 8:12], ACT.Sqrt, bias=eps, scale=1.0 / ROPE).then_inc(sem("msd"), 1)
                        act.wait_ge(sem("my"), n + 1)
                        fn(V[:, t, hb * 256:(hb + 1) * 256].rearrange("p (h x) -> p h x", h=4), kv[:, :, NOPE:],
                           ACT.Identity).then_inc(sem("mvev"), 1)
                        if t:
                            turned(n - 1)
                    turned(hb * T + T - 1)
                    attention(1, 8 * hb, 8 * hb + 8)

            def gate(l):
                act.wait_ge(sem("gl"), l + 1)
                v = view(SCR, 0, T, G)
                fn(v, v, ACT.Exp).then_inc(sem("gle"), 1)
                act.wait_ge(sem("el"), l + 1)
                v = view(SCR, 512, T, EPG)
                fn(v, v, ACT.Exp).then_inc(sem("ele"), 1)

            def expert_step(l, b, n, before):
                act.wait_ge(sem(f"xt{l}"), n + 1)
                wait(act, sem(f"b{l}"), before)
                for c in range(0, C, 2):
                    last = fn(xgT[b][:, c, :], PB[0][:, (c // 2) * P:(c // 2 + 1) * P], ACT.Identity,
                              bias=MODC[:, l, 2, c:c + 1], scale=GC[:, 2 * l + 1, c:c + 1])
                last.then_inc(sem(f"xA{l}"), 1)
                act.wait_ge(sem(f"a{l}"), n + 1)
                wait(act, sem(f"hid{l}"), n)
                fn(sil, PB[2][:, 0:FF], ACT.Silu).then_inc(sem(f"sil{l}"), 1)
                act.wait_ge(sem(f"ht{l}"), n + 1)
                wait(act, sem(f"y{l}"), n)
                fn(hidT, PB[4][:, 0:2 * P].rearrange("p (a q) -> p a q", a=2), ACT.Identity).then_inc(sem(f"hT{l}"), 1)
                act.wait_ge(sem(f"y{l}"), n + 1)

            def expert_out(l, b, q):
                wait(act, sem(f"scat{l}{b}"), 16 * q)
                fn(ysb[b][:, 0:NH], PB[5][:, :], ACT.Identity).then_inc(sem(f"yA{l}"), 1)

            def experts(l):
                for b in range(2):
                    expert_step(l, b, b, b - 1)
                    expert_out(l, b, 0)
                with act.Fori(1, PAIRS // 2) as i:
                    for b in range(2):
                        expert_step(l, b, 2 * i + b, 2 * i + b - 1)
                        expert_out(l, b, i)
                act.wait_ge(sem("ctl"), l + 1)
                tails = act.value_load(CTL[0:1, 0:1], min_val=0, max_val=TAILS)
                with act.Fori(0, TAILS) as j:
                    with act.If(j < tails):
                        expert_step(l, 0, PAIRS + j, PAIRS + j)
                        expert_out(l, 0, PAIRS // 2 + j)

            norm(0)
            modulate(0)
            da_project()
            attention(0, 0, 32)
            output_norm()
            output_turn(0)
            norm(1)
            modulate(1)
            gate(0)
            experts(0)
            norm(2)
            modulate(2)
            latents()
            mla()
            output_turn(1)
            norm(3)
            modulate(3)
            gate(1)
            experts(1)

        @block.vector
        def _(dve):
            v = nc.vector
            chain = Chain(dve, sem("dve"))
            link = chain.link
            tt, ts, stt, red = v.tensor_tensor, v.tensor_scalar, v.scalar_tensor_tensor, v.tensor_reduce

            def over(ap, axis, n):
                ap = ap.unsqueeze(axis)
                shape = list(ap.shape)
                shape[axis] = n
                return ap.broadcast_to(shape)

            v.memset(eps, EPS).then_inc(sem("dve"), 1)
            chain.n += 1
            dve.wait_ge(sem("in"), 16 * N_IN)
            dve.wait_ge(sem("silc"), 1)
            v.tensor_copy(condr, over(cc, 2, 32)).then_inc(sem("cond"), 1)
            lp = view(RV, 0, 2, DH)
            link(tt(lp, lamv[:, 0:4:2], lamv[:, 1:4:2], ALU.mult))
            red(lam[:, 0:2], lp, AX.X, ALU.add).then_inc(sem("lams"), 1)
            ang, kk, half = view(RH, 0, T, 48), view(RH, 512, T, 48), view(RH, 1024, T, 48)
            link(v.tensor_copy(posf, posi[:, :]))
            link(tt(ang, over(posf, 2, 48), over(invs, 1, T), ALU.mult))
            link(ts(kk, ang, 1.0 / TWO_PI, None, ALU.mult))
            link(ts(kk, kk, MAGIC, None, ALU.add))
            link(ts(kk, kk, MAGIC, None, ALU.subtract))
            for part in (PI_A, PI_B, PI_C):
                link(stt(ang, kk, -part, ang, ALU.mult, ALU.add))
            ts(ang, ang, math.pi * (1 - 1e-7), -math.pi * (1 - 1e-7), ALU.min, ALU.max).then_inc(sem("ang"), 1)
            dve.wait_ge(sem("lame"), 1)
            link(tt(lam[:, 2:3], lam[:, 1:2], lam[:, 0:1], ALU.subtract))
            link(ts(lam[:, 3:4], lam[:, 2:3], -LAMBDA_INIT, None, ALU.add))
            link(ts(subc, subc, 1.0 - LAMBDA_INIT, None, ALU.mult))
            dve.wait_ge(sem("sin"), 1)
            sn, cs = view(RH, 2048, T, 48), view(RH, 2560, T, 48)
            link(tt(cs, cs, cs, ALU.mult))
            link(ts(cs, cs, -2.0, 1.0, ALU.mult, ALU.add))
            for tab, half_dim, at, g0 in ((DT, DH // 2, 0, 0), (RT, ROPE // 2, DH // 2, 2 * DH)):
                n = half_dim
                for w in range(2):
                    g1 = gnb[:, g0 + 2 * n * w:g0 + 2 * n * w + n]
                    g2 = gnb[:, g0 + 2 * n * w + n:g0 + 2 * n * (w + 1)]
                    si, co = sn[:, :, at:at + n], cs[:, :, at:at + n]
                    tt(tab[:, :, 2 * w, 0:n], co, over(g1, 1, T), ALU.mult)
                    tt(tab[:, :, 2 * w, n:], co, over(g2, 1, T), ALU.mult)
                    link(tt(tab[:, :, 2 * w + 1, 0:n], si, over(g2, 1, T), ALU.mult))
                    tt(tab[:, :, 2 * w + 1, n:], si, over(g1, 1, T), ALU.mult)
                    link(ts(tab[:, :, 2 * w + 1, 0:n], tab[:, :, 2 * w + 1, 0:n], -1.0, None, ALU.mult))

            def ada_out(a):
                dve.wait_ge(sem("ada"), 8 * a + 8)
                dve.wait_ge(sem("ab"), 64 * (a + 1))
                tt(MR[:, :], MR[:, :], PB[5 + a % 2][:, :], ALU.add).then_inc(sem("mr"), 1)

            def gains(k):
                l, w = divmod(k, 2)
                dve.wait_ge(sem("mc"), 16 * (4 * l + 2 * w + 2))
                stt(GC[:, k], MODC[:, l, 2 * w + 1], 1.0, NRM[:, w, l], ALU.add, ALU.mult).then_inc(sem("gc"), 1)

            def norm(k):
                for t in range(T):
                    dve.wait_ge(sem("sd"), 4 * k + t + 1)
                    if t == 0 and k in (1, 3):
                        dve.wait_ge(sem("wo"), 2 * T * (k // 2 + 1))
                    if t == 0 and k == 2:
                        dve.wait_ge(sem("comb"), T)
                    link(v.reciprocal(rs[:, t:t + 1], sd[:, t:t + 1]))
                    ts(XN[:, t, :].rearrange("p (c m) -> p c m", c=C), X[:, t, :].rearrange("p (m c) -> p c m", c=C),
                       rs[:, t:t + 1], None, ALU.mult).then_inc(sem("xn"), 1)

            def modulate(k):
                l, w = divmod(k, 2)
                dve.wait_ge(sem("gc"), k + 1)
                dve.wait_ge(sem("xt"), 4 * k + 4)
                for c in range(1, C, 2):
                    ts(HT[:, c, :], PB[c][:, :], GC[:, k, c:c + 1], MODC[:, l, 2 * w, c:c + 1], ALU.mult,
                       ALU.add).then_inc(sem("hD"), 1)

            def da_project():
                def step(hb, n12, n):
                    w, t = divmod(n12, T)
                    if w == 2:
                        return
                    m = hb * 8 + n12
                    b = m % 2
                    dve.wait_ge(sem("dsq"), m + 1)
                    wait(dve, sem("dsd"), m - 1)
                    red(hss[:, b, 0:8], SQ.rearrange("p (h x) -> p h x", h=8), AX.X, ALU.add).then_inc(sem("dss"), 1)
                    dve.wait_ge(sem("dsd"), m + 1)
                    wait(dve, sem("day"), m)
                    v.reciprocal(hrs[:, b, 0:8], hsd[:, b, 0:8]).then_inc(sem("drs"), 1)
                    dve.wait_ge(sem("drs"), m + 1)
                    wait(dve, sem("dat"), m)
                    src = PB[n % 4][:, :].rearrange("p (h x) -> p h x", h=8)
                    m1, m2 = view(M1, 0, 8, DH), view(M2, 0, 8, DH)
                    cos, sin = DT[:, t, 2 * w], DT[:, t, 2 * w + 1]
                    nn = DH // 2
                    tt(m1, src, over(cos, 1, 8), ALU.mult)
                    tt(m2[:, :, 0:nn], src[:, :, nn:], over(sin[:, 0:nn], 1, 8), ALU.mult)
                    wait(dve, sem("daev"), n)
                    tt(m2[:, :, nn:], src[:, :, 0:nn], over(sin[:, nn:], 1, 8), ALU.mult).then_inc(sem("daev"), 1)
                    dve.wait_ge(sem("daev"), n + 1)
                    link(tt(m1, m1, m2, ALU.add))
                    tt(YT.rearrange("p (h x) -> p h x", h=8), m1, over(hrs[:, b, 0:8], 2, DH),
                       ALU.mult).then_inc(sem("day"), 1)

                for n in range(24):
                    step(*divmod(n, 12), n)
                    for u in ada_after(n):
                        if u % C == C - 1:
                            ada_out(u // C)

            def attention(l, i0, i1):
                scale = DH ** -0.5 if l == 0 else QK ** -0.5

                def maxima(i):
                    t, b, n = i % T, i % 2, 32 * l + i
                    L = (t + 1) * P
                    dve.wait_ge(sem("sc"), n + 1)
                    wait(dve, sem("exp"), n - 1)
                    wait(dve, sem("nm"), n)
                    for a in range(2):
                        last = red(mx[:, b, a:a + 1], PB[2 * b + a][:, 0:L], AX.X, ALU.max)
                    link(last)
                    ts(nmx[:, b], mx[:, b], -scale, None, ALU.mult).then_inc(sem("nm"), 1)

                def normalise(i):
                    t, b, n = i % T, i % 2, 32 * l + i
                    L = (t + 1) * P
                    dve.wait_ge(sem("exp"), n + 1)
                    wait(dve, sem("p"), n)
                    if l == 0:
                        link(v.reciprocal(ls[:, b], ls[:, b]))
                        v.tensor_scalar(rl[:, b, 1:2], ls[:, b, 1:2], lam[:, 3:4], None, ALU.mult)
                        link(ts(pr[b][:, 0, 0:L], pr[b][:, 0, 0:L], ls[:, b, 0:1], None, ALU.mult))
                        stt(pr[b][:, 0, 0:L], pr[b][:, 1, 0:L], rl[:, b, 1:2], pr[b][:, 0, 0:L], ALU.mult,
                            ALU.add).then_inc(sem("p"), 1)
                    else:
                        wait(dve, sem("oe"), n - 1)
                        v.reciprocal(rl[:, b], ls[:, b]).then_inc(sem("p"), 1)

                def turned(i):
                    t, b, n = i % T, i % 2, 32 * l + i
                    L = (t + 1) * P
                    if l == 1:
                        dve.wait_ge(sem("tr"), n + 1)
                        wait(dve, sem("av"), n - 1)
                        v.tensor_copy(aT[b][:, 1, 0:L], PB[5][:, 0:L]).then_inc(sem("tev1"), 1)

                def output(i):
                    (g, t), b, n = divmod(i, T), i % 2, 32 * l + i
                    dve.wait_ge(sem("av"), n + 1)
                    tt(OTOK[:, t, g * P:(g + 1) * P].rearrange("p (a x) -> p a x", a=2),
                       PB[6 + b][:, 0:P].rearrange("p (a x) -> p a x", a=2), over(rl[:, b], 2, VD),
                       ALU.mult).then_inc(sem("oe"), 1)

                maxima(i0)
                maxima(i0 + 1)
                for i in range(i0, i1):
                    normalise(i)
                    if i + 2 < i1:
                        maxima(i + 2)
                    turned(i)
                    if l == 1 and i > i0:
                        output(i - 1)
                if l == 1:
                    output(i1 - 1)

            def output_norm():
                for t in range(T):
                    o = slice(8 * t, 8 * t + 8)
                    dve.wait_ge(sem("osq"), t + 1)
                    red(hss[:, 0, o], view(PS, 0, DA_H, P), AX.X, ALU.add).then_inc(sem("oss"), 1)
                    dve.wait_ge(sem("osd"), t + 1)
                    link(v.reciprocal(hrs[:, 0, o], hsd[:, 0, o]))
                    ot = OTOK[:, t, :].rearrange("p (h x) -> p h x", h=DA_H)
                    tt(ot, ot, over(hrs[:, 0, o], 2, P), ALU.mult).then_inc(sem("on"), 1)

            def residual(l):
                dve.wait_ge(sem(f"gm{l}"), 16)
                for t in range(T):
                    for n in range(2):
                        m = 8 * l + 2 * t + n
                        dve.wait_ge(sem("wo"), m + 1)
                        tmp = view(PS, 1024 + NH * (n % 2), NH)
                        cols = slice(n * NH, (n + 1) * NH)
                        tt(tmp, PB[2 * t + n][:, :], GM[:, cols], ALU.mult).then_inc(sem("oev"), 1)
                        dve.wait_ge(sem("oev"), m + 1)
                        last = tt(X[:, t, cols], X[:, t, cols], tmp, ALU.add)
                        if n == 0:
                            link(last)
                        else:
                            last.then_inc(sem("res"), 1)
                            dve.wait_ge(sem("res"), 4 * l + t + 1)

            def first_max(oh, s, width, iota_, tmp):
                m, cand = tmp
                link(red(m, s, AX.X, ALU.max))
                link(tt(oh, s, over(m, 2, width), ALU.is_ge))
                link(ts(cand, oh, -100.0, None, ALU.mult))
                link(tt(cand, cand, over(iota_, 1, T), ALU.add))
                link(red(m, cand, AX.X, ALU.min))
                link(tt(oh, cand, over(m, 2, width), ALU.is_equal))

            def gate(l):
                R = {}
                at = [0]

                def r(*shape):
                    x = view(SCR, at[0], *shape)
                    at[0] += math.prod(shape)
                    assert at[0] <= 4096
                    return x
                gl = view(SCR, 0, T, G)
                M = view(SCR, 256, T, E)
                el = view(SCR, 512, T, EPG)
                at[0] = 640
                m4, gb, ohg, cg = r(T), r(T, G), r(T, G), r(T, G)
                gate_, br, es, cand, oh1, oh2, tmp8 = r(T), r(T, EPG), r(T, EPG), r(T, EPG), r(T, EPG), r(T, EPG), r(T, EPG)
                s1 = r(T)
                LG = r(T, NR)
                sel = r(T * EPG, G)
                OH = r(T, 2, E)
                tmp = r(T, 2, E)
                rank, slot, slotf = r(T, E), r(T, E), r(T, 2)
                cnt, extra, cum, base, ge = r(E), r(E), r(E), r(E), r(T, E)
                cmp7 = r(E, 7)
                tailf = r(1 + 2 * TAILS)
                at[0] = 2816
                lt = r(E, E)
                dve.wait_ge(sem("lg"), l + 1)
                dve.wait_ge(sem("bgr"), 32 * (l + 1))
                dve.wait_ge(sem("lt"), 2 * (l + 1))
                link(v.tensor_copy(LG, PB[0][:, 0:T * NR].rearrange("p (t n) -> p t n", t=T)))
                link(red(m4, LG[:, :, 0:G], AX.X, ALU.max))
                tt(gl, LG[:, :, 0:G], over(m4, 2, G), ALU.subtract).then_inc(sem("gl"), 1)
                dve.wait_ge(sem("gle"), l + 1)
                link(red(m4, gl, AX.X, ALU.add))
                link(v.reciprocal(m4, m4))
                link(tt(gl, gl, over(m4, 2, G), ALU.mult))
                link(tt(gb, gl, over(bgr[:, 0:G], 1, T), ALU.add))
                first_max(ohg, gb, G, i8[:, 0:G], (m4, cg))
                link(tt(cg, gl, ohg, ALU.mult))
                link(red(gate_, cg, AX.X, ALU.add))
                sel4 = sel.rearrange("p (t e) g -> p t e g", t=T)
                link(tt(sel4, LG[:, :, G:].rearrange("p t (g e) -> p t e g", g=G), over(ohg, 2, EPG), ALU.mult))
                link(red(el, sel4, AX.X, ALU.add))
                link(tt(sel4, over(bgr[:, G:].rearrange("p (g e) -> p e g", g=G), 1, T), over(ohg, 2, EPG), ALU.mult))
                link(red(br, sel4, AX.X, ALU.add))
                link(red(m4, el, AX.X, ALU.max))
                tt(el, el, over(m4, 2, EPG), ALU.subtract).then_inc(sem("el"), 1)
                dve.wait_ge(sem("ele"), l + 1)
                link(red(m4, el, AX.X, ALU.add))
                link(v.reciprocal(m4, m4))
                link(tt(el, el, over(m4, 2, EPG), ALU.mult))
                link(tt(es, el, br, ALU.add))
                first_max(oh1, es, EPG, i8, (m4, cand))
                link(ts(tmp8, oh1, NEG, None, ALU.mult))
                link(tt(es, es, tmp8, ALU.add))
                first_max(oh2, es, EPG, i8, (m4, cand))
                for k, oh in enumerate((oh1, oh2)):
                    for g in range(G):
                        last = tt(OH[:, :, k, g * EPG:(g + 1) * EPG], oh, over(ohg[:, :, g], 2, EPG), ALU.mult)
                link(last)
                tt(M, OH[:, :, 0], OH[:, :, 1], ALU.add).then_inc(sem("M"), 1)
                for k, oh in enumerate((oh1, oh2)):
                    link(tt(tmp8, el, oh, ALU.mult))
                    link(red(Wt[:, :, k], tmp8, AX.X, ALU.add))
                link(tt(s1, Wt[:, :, 0], Wt[:, :, 1], ALU.add))
                link(v.reciprocal(s1, s1))
                link(tt(s1, s1, gate_, ALU.mult))
                link(tt(Wt, Wt, over(s1, 2, 2), ALU.mult))
                dve.wait_ge(sem("rank"), l + 1)
                link(v.tensor_copy(rank, PB[1][:, 0:T * E].rearrange("p (t e) -> p t e", t=T)))
                link(v.tensor_copy(cnt, PB[1][:, T * E:(T + 1) * E]))
                link(tt(cmp7, over(cnt, 2, 7), over(th, 1, E), ALU.is_gt))
                link(red(extra, cmp7, AX.X, ALU.add))
                link(tt(lt, lt, over(extra, 1, E), ALU.mult))
                link(red(cum, lt, AX.X, ALU.add))
                link(ts(base, cum, float(CAP), float(E * CAP - CAP), ALU.mult, ALU.add))
                link(stt(base, i32f, -float(CAP), base, ALU.mult, ALU.add))
                link(ts(ge, rank, float(CAP), None, ALU.is_ge))
                link(tt(ge, ge, over(base, 1, T), ALU.mult))
                link(tt(slot, rank, ge, ALU.add))
                link(ts(base, i32f, float(CAP), None, ALU.mult))
                link(tt(slot, slot, over(base, 1, T), ALU.add))
                link(tt(tmp, OH, over(slot, 2, 2), ALU.mult))
                link(red(slotf, tmp, AX.X, ALU.add))
                v.tensor_copy(sloti[:, :, :], slotf).then_inc(sem("slot"), 1)
                link(tt(extra, extra, cum, ALU.add))
                o16 = view(SCR, 2816, 2 * TAILS, E)
                o16b = view(SCR, 2816 + 2 * TAILS * E, 2 * TAILS, E)
                link(tt(o16, over(i16f, 2, E), over(cum, 1, 2 * TAILS), ALU.is_ge))
                link(tt(o16b, over(i16f, 2, E), over(extra, 1, 2 * TAILS), ALU.is_lt))
                link(tt(o16, o16, o16b, ALU.mult))
                link(tt(o16, o16, over(i32f, 1, 2 * TAILS), ALU.mult))
                link(red(tailf[:, 1:], o16, AX.X, ALU.add))
                link(ts(cmp7[:, 0, 0:1], extra[:, E - 1:E], 1.0, None, ALU.mult))
                link(tt(o16[:, 0, 0:TAILS], i16f[:, 0:2 * TAILS:2], cmp7[:, 0, 0:1].broadcast_to([P, TAILS]), ALU.is_lt))
                link(red(tailf[:, 0:1], o16[:, 0, 0:TAILS], AX.X, ALU.add))
                v.tensor_copy(CTL[:, :], tailf[0:1, :]).then_inc(sem("ctl"), 1)
                dve.wait_ge(sem("tabl"), 16 * (l + 1))
                ts(idx[:, 1, :], idx[:, 0, :], 1, None, ALU.logical_shift_right).then_inc(sem("idx"), 1)

            def expert_step(l, b, q, n, before):
                dve.wait_ge(sem(f"xt{l}"), n + 1)
                wait(dve, sem(f"b{l}"), before)
                for c in range(1, C, 2):
                    last = ts(xgT[b][:, c, :], PB[1][:, (c // 2) * P:(c // 2 + 1) * P], GC[:, 2 * l + 1, c:c + 1],
                              MODC[:, l, 2, c:c + 1], ALU.mult, ALU.add)
                last.then_inc(sem(f"xD{l}"), 1)
                dve.wait_ge(sem(f"b{l}"), n + 1)
                dve.wait_ge(sem(f"sil{l}"), n + 1)
                wait(dve, sem(f"ht{l}"), n)
                tt(hid, sil.rearrange("p (m c) -> p c m", c=2), PB[3][:, 0:FF].rearrange("p (m c) -> p c m", c=2),
                   ALU.mult).then_inc(sem(f"hid{l}"), 1)
                dve.wait_ge(sem(f"y{l}"), n + 1)
                wait(dve, sem(f"scat{l}{b}"), 16 * q)
                v.tensor_copy(ysb[b][:, NH:], PB[6][:, :]).then_inc(sem(f"yD{l}"), 1)

            def experts(l):
                for b in range(2):
                    expert_step(l, b, 0, b, b - 1)
                with dve.Fori(1, PAIRS // 2) as i:
                    for b in range(2):
                        expert_step(l, b, i, 2 * i + b, 2 * i + b - 1)
                dve.wait_ge(sem("ctl"), l + 1)
                tails = dve.value_load(CTL[0:1, 0:1], min_val=0, max_val=TAILS)
                with dve.Fori(0, TAILS) as j:
                    with dve.If(j < tails):
                        expert_step(l, 0, PAIRS // 2 + j, PAIRS + j, PAIRS + j)

            def combine(l):
                dve.wait_ge(sem(f"gf{l}"), 16)
                for t in range(T):
                    dve.wait_ge(sem(f"yl{t}"), 16 * (l + 1))
                    y = YP[t]
                    link(ts(y[:, 0], y[:, 0], Wt[:, t, 0:1], None, ALU.mult))
                    link(stt(y[:, 0], y[:, 1], Wt[:, t, 1:2], y[:, 0], ALU.mult, ALU.add))
                    link(tt(y[:, 0], y[:, 0], GF[:, :], ALU.mult))
                    tt(X[:, t, :], X[:, t, :], y[:, 0], ALU.add).then_inc(sem("comb"), 1)

            def latents():
                for t in range(T):
                    o = [PB[2 * (t % 2)], PB[2 * (t % 2) + 1]]
                    dve.wait_ge(sem("lsd"), t + 1)
                    v.reciprocal(rs[:, 4:7], sd[:, 4:7]).then_inc(sem("lrs"), 1)
                    dve.wait_ge(sem("lrs"), t + 1)
                    wait(dve, sem("ltt"), t)
                    ts(LT_[:, 0:QR], o[0][:, 0:QR], rs[:, 4:5], None, ALU.mult)
                    ts(LT_[:, QR:], o[1][:, 0:KVR], rs[:, 5:6], None, ALU.mult).then_inc(sem("ln"), 1)
                    src = o[1][:, KVR:KVR + ROPE].unsqueeze(1)
                    rotate2(KP[:, t, :], src, RT[:, t, 2], RT[:, t, 3], t)
                    if t:
                        turn_latents(t - 1)
                turn_latents(T - 1)

            def rotate2(dst, src, cos, sin, t):
                n = ROPE // 2
                m1, m2 = view(PS, 2048, 1, ROPE), view(PS, 2048 + ROPE, 1, ROPE)
                tt(m1, src, over(cos, 1, 1), ALU.mult)
                tt(m2[:, :, 0:n], src[:, :, n:], over(sin[:, 0:n], 1, 1), ALU.mult)
                tt(m2[:, :, n:], src[:, :, 0:n], over(sin[:, n:], 1, 1), ALU.mult).then_inc(sem("lev"), 1)
                dve.wait_ge(sem("lev"), t + 1)
                link(tt(m1, m1, m2, ALU.add))
                link(ts(dst, m1[:, 0], rs[:, 6:7], None, ALU.mult))

            def turn_latents(t):
                dve.wait_ge(sem("ltt"), t + 1)
                for k in range(KVC):
                    last = ts(CT[:, QRC + k, t * P:(t + 1) * P], PB[5][:, k * P:(k + 1) * P], kvan[:, k:k + 1], None, ALU.mult)
                last.then_inc(sem("ltevD"), 1)

            def mla():
                def turned(n):
                    hb, t = divmod(n, T)
                    dve.wait_ge(sem("mt"), n + 1)
                    wait(dve, sem("sc"), 32 + 8 * (hb - 1))
                    ts(mk[hb % 2][0:QK, :, t * P:(t + 1) * P], PB[5][0:QK, :].rearrange("p (h q) -> p h q", h=4),
                       knc[0:QK, :], None, ALU.mult).then_inc(sem("mtevD"), 1)

                for hb in range(4):
                    for t in range(T):
                        n = hb * T + t
                        sq, sk = view(PS, 0, 4, QK), view(PS, 4 * QK, 4, NOPE)
                        q = PB[n % 2][:, 0:4 * QK].rearrange("p (h x) -> p h x", h=4)
                        kv = PB[2 + n % 2][:, :].rearrange("p (h x) -> p h x", h=4)
                        dve.wait_ge(sem("msq"), n + 1)
                        wait(dve, sem("msd"), n)
                        red(hss[:, 0, 0:4], sq[:, :, 0:NOPE], AX.X, ALU.add)
                        red(hss[:, 0, 8:12], sq[:, :, NOPE:], AX.X, ALU.add)
                        red(hss[:, 0, 4:8], sk, AX.X, ALU.add).then_inc(sem("mss"), 1)
                        dve.wait_ge(sem("msd"), n + 1)
                        wait(dve, sem("my"), n)
                        v.reciprocal(hrs[:, 0, 0:12], hsd[:, 0, 0:12]).then_inc(sem("mrs"), 1)
                        dve.wait_ge(sem("mrs"), n + 1)
                        wait(dve, sem("mt"), n)
                        nn = ROPE // 2
                        m1, m2 = view(PS, 2048, 4, ROPE), view(PS, 2048 + 128, 4, ROPE)
                        qp = q[:, :, NOPE:]
                        cos, sin = RT[:, t, 0], RT[:, t, 1]
                        tt(QY[:, :, 0:NOPE], q[:, :, 0:NOPE], over(hrs[:, 0, 0:4], 2, NOPE), ALU.mult)
                        tt(m1, qp, over(cos, 1, 4), ALU.mult)
                        tt(m2[:, :, 0:nn], qp[:, :, nn:], over(sin[:, 0:nn], 1, 4), ALU.mult)
                        tt(m2[:, :, nn:], qp[:, :, 0:nn], over(sin[:, nn:], 1, 4), ALU.mult).then_inc(sem("mev"), 1)
                        tt(KY[:, :, 0:NOPE], kv[:, :, 0:NOPE], over(hrs[:, 0, 4:8], 2, NOPE), ALU.mult)
                        v.tensor_copy(KY[:, :, NOPE:], over(KP[:, t, :], 1, 4))
                        dve.wait_ge(sem("mev"), n + 1)
                        link(tt(m1, m1, m2, ALU.add))
                        tt(QY[:, :, NOPE:], m1, over(hrs[:, 0, 8:12], 2, ROPE), ALU.mult).then_inc(sem("my"), 1)
                        if t:
                            turned(n - 1)
                    turned(hb * T + T - 1)
                    attention(1, 8 * hb, 8 * hb + 8)

            ada_out(0)
            gains(0)
            norm(0)
            modulate(0)
            da_project()
            gains(1)
            attention(0, 0, 32)
            output_norm()
            residual(0)
            norm(1)
            modulate(1)
            gate(0)
            experts(0)
            gains(2)
            combine(0)
            norm(2)
            modulate(2)
            latents()
            mla()
            gains(3)
            residual(1)
            norm(3)
            modulate(3)
            gate(1)
            experts(1)
            combine(1)

        @block.gpsimd
        def _(pool):
            g = nc.gpsimd
            g.memset(ones[:, :], 1.0)
            g.memset(ident[:, :], 0.0)
            g.memset(mneg[:, :], 0.0)
            tabinit = view(RQK, 0, NSLOT // P).bitcast(I32)
            g.memset(tabinit, NOWHERE)
            g.memset(tri[:, :], 1.0).then_inc(sem("pool"), 1)
            pool.wait_ge(sem("pool"), 1)
            g.affine_select(out=ident[:, :], in_=ident[:, :], compare_op=ALU.not_equal, fill=1.0, base=0,
                            pattern=[[-1, P]], channel_multiplier=1).then_inc(sem("const"), 1)
            g.affine_select(out=tri[:, :], in_=tri[:, :], compare_op=ALU.is_gt, fill=0.0, base=0,
                            pattern=[[1, P]], channel_multiplier=-1).then_inc(sem("const"), 1)
            g.affine_select(out=mneg[:, :], in_=mneg[:, :], compare_op=ALU.is_ge, fill=NEG, base=0,
                            pattern=[[-1, P]], channel_multiplier=1).then_inc(sem("const"), 1)
            g.iota(pid[:, :, :], [[2 * P, T], [1, 2]], base=0, channel_multiplier=2)
            g.iota(i8, [[1, EPG]], base=0, channel_multiplier=0, allow_small_or_imprecise_dtypes=True)
            g.iota(i32f, [[1, E]], base=0, channel_multiplier=0, allow_small_or_imprecise_dtypes=True)
            g.iota(i16f, [[1, 2 * TAILS]], base=0, channel_multiplier=0, allow_small_or_imprecise_dtypes=True)
            g.iota(th, [[CAP, 7]], base=CAP, channel_multiplier=0, allow_small_or_imprecise_dtypes=True).then_inc(sem("pool"), 1)
            pool.wait_ge(sem("pool"), 2)
            g.memset(qnc[NOPE:QK, :], 1.0)
            g.memset(knc[NOPE:QK, :], 1.0).then_inc(sem("pool"), 1)
            for l in range(2):
                pool.dma_start(tab_d[l][:, :].rearrange("(p n) o -> p (n o)", p=P), tabinit).then_inc(sem("tabi"), 16)

            def router_weights(l):
                with nc.allow_non_contiguous_dma(reason="narrow router weights"):
                    pool.dma_start(WGR[:, :, 0:G], A["moe_w_group"][l].rearrange("(p c) n -> p c n", c=C)).then_inc(sem("wgr"), 16)
                    pool.dma_start(WGR[:, :, G:], A["moe_w_router"][l].rearrange("(p c) n -> p c n", c=C)).then_inc(sem("wgr"), 16)
                    pool.dma_start(bgr[:, 0:G], A["moe_b_group"][l].partition_broadcast(P)).then_inc(sem("bgr"), 16)
                    pool.dma_start(bgr[:, G:], A["moe_b_router"][l].rearrange("g e -> (g e)").partition_broadcast(P)).then_inc(sem("bgr"), 16)

            def bias_rows(a):
                l, gr = divmod(a, 3)
                wait(pool, sem("mo"), 16 * a)
                for j in range(4):
                    n = (4 * gr + j) * NH
                    pool.dma_start(MR[32 * j:32 * j + 32, :], A["ada_b"][l, n:n + NH].partition_broadcast(32)).then_inc(sem("ab"), 16)

            columns = [0]

            def column(dst, l, w):
                src = mod_d[l, w * D:(w + 1) * D].rearrange("(p c) -> p c", c=C)
                with nc.allow_non_contiguous_dma(reason="a vector by partition"):
                    pool.dma_start(dst, src).then_inc(sem("mc"), 16)
                columns[0] += 1
                pool.wait_ge(sem("mc"), 16 * columns[0])

            def gate_row(l, w):
                dst, s = (GM, f"gm{l}") if w == 2 else (GF, f"gf{l}")
                pool.dma_start(dst[:, :], mod_d[l, w * D:(w + 1) * D].partition_broadcast(P)).then_inc(sem(s), 16)

            def mod_group(a):
                l, gr = divmod(a, 3)
                pool.wait_ge(sem("mr"), a + 1)
                pool.dma_start(mod_d[l, gr * 2 * D:(gr + 1) * 2 * D].rearrange("(j n) -> j n", j=4),
                               MR[0:P:32, :]).then_inc(sem("mo"), 16)
                pool.wait_ge(sem("mo"), 16 * (a + 1))
                if a < 5:
                    bias_rows(a + 1)
                if gr == 0:
                    column(MODC[:, l, 0], l, 0)
                    column(MODC[:, l, 1], l, 1)
                elif gr == 1:
                    column(MODC[:, l, 2], l, 3)
                    if l == 0:
                        gate_row(0, 2)
                else:
                    column(MODC[:, l, 3], l, 4)
                    if l == 0:
                        gate_row(0, 5)

            last_token, last_pair = pool.to_reg(S - 1), pool.to_reg(2 * S - 1)
            bias_rows(0)
            router_weights(0)
            mod_group(0)
            pool.wait_ge(sem("tabi"), 32)
            pool.wait_ge(sem("pool"), 3)
            g.memset(dak[0][64:P, :, :], 0.0).then_inc(sem("pool"), 1)
            pool.wait_ge(sem("pool"), 4)
            g.memset(dak[1][0:64, :, :], 0.0).then_inc(sem("pool"), 1)
            pool.wait_ge(sem("pool"), 5)
            for a in range(1, 6):
                mod_group(a)

            def settle():
                pool.sem_inc(sem("pool_turns"), 1)

            def layer(l):
                for t in range(T):
                    pool.wait_ge(sem("xn"), 4 * (2 * l + 1) + t + 1)
                    pool.dma_start(xn_d[l][t * P:(t + 1) * P, :], XN[:, t, :]).then_inc(sem("xd"), 16)
                if l == 0:
                    gate_row(1, 2)
                lt = view(SCR, 2816, E, E)
                pool.wait_ge(sem("av"), 32 * (l + 1))
                g.memset(lt, 1.0).then_inc(sem("lt"), 1)
                pool.wait_ge(sem("lt"), 2 * l + 1)
                g.affine_select(out=lt, in_=lt, compare_op=ALU.is_gt, fill=0.0, base=0,
                                pattern=[[1, E], [-1, E]], channel_multiplier=0).then_inc(sem("lt"), 1)
                g.memset(xg[0], 0.0)
                g.memset(xg[1], 0.0).then_inc(sem("xg0"), 1)
                pool.wait_ge(sem("slot"), l + 1)
                pool.wait_ge(sem("pool"), 2)
                for t in range(T):
                    for k in range(2):
                        pool.indirect_dma_start(tab_d[l][:, :], bass.IndirectOffsetOnAxis(ap=sloti[:, t, k:k + 1], axis=0),
                                                pid[:, t, k:k + 1], None).then_inc(sem("tabs"), 16)
                pool.wait_ge(sem("tabs"), 16 * 2 * T * (l + 1))
                with nc.allow_non_contiguous_dma(reason="the slot table"):
                    pool.dma_start(idx[:, 0, :], tab_d[l][:, :].rearrange("(n p) o -> p (n o)", p=P)).then_inc(sem("tabl"), 16)
                pool.wait_ge(sem("xg0"), l + 1)

                def gather(b, q, n, before):
                    wait(pool, sem(f"xt{l}"), before)
                    wait(pool, sem(f"gath{l}{b}"), 16 * q)
                    pool.wait_ge(sem("idx"), l + 1)
                    g.tensor_copy(ci[:, b:b + 1], idx[:, 1, bass.ds(n, 1)]).then_inc(sem(f"gi{l}"), 1)
                    pool.wait_ge(sem(f"gi{l}"), n + 1)
                    settle()
                    pool.wait_ge(sem("xd"), 16 * T * (l + 1))
                    pool.indirect_dma_start(xg[b], None, xn_d[l][:, :],
                                            bass.IndirectOffsetOnAxis(ap=ci[:, b:b + 1], axis=0), bounds_check=last_token,
                                            oob_is_err=False).then_inc(sem(f"gath{l}{b}"), 16)

                def scatter(b, q, n):
                    wait(pool, sem(f"scat{l}{b}"), 16 * q)
                    pool.wait_ge(sem("idx"), l + 1)
                    g.tensor_copy(ci[:, 2 + b:3 + b], idx[:, 0, bass.ds(n, 1)]).then_inc(sem(f"si{l}"), 1)
                    pool.wait_ge(sem(f"si{l}"), n + 1)
                    pool.wait_ge(sem(f"yA{l}"), n + 1)
                    pool.wait_ge(sem(f"yD{l}"), n + 1)
                    settle()
                    pool.indirect_dma_start(y_d[l][:, :], bass.IndirectOffsetOnAxis(ap=ci[:, 2 + b:3 + b], axis=0),
                                            ysb[b], None, bounds_check=last_pair, oob_is_err=False).then_inc(sem(f"scat{l}{b}"), 16)

                def turn(i):
                    for b in range(2):
                        scatter(b, i, 2 * i + b)
                        gather(b, i + 1, 2 * i + 2 + b, 2 * i + b + 1)

                half = PAIRS // 2
                for b in range(2):
                    gather(b, 0, b, 0)
                turn(0)
                with pool.Fori(1, half - 1) as i:
                    turn(i)
                for b in range(2):
                    scatter(b, half - 1, PAIRS - 2 + b)
                pool.wait_ge(sem("ctl"), l + 1)
                tails = pool.value_load(CTL[0:1, 0:1], min_val=0, max_val=TAILS)
                with pool.Fori(0, TAILS) as j:
                    with pool.If(j < tails):
                        gather(0, half + j, PAIRS + j, PAIRS + j)
                        scatter(0, half + j, PAIRS + j)
                pool.wait_ge(sem(f"scat{l}1"), 16 * half)
                pool.wait_ge(sem(f"scat{l}0"), tails * 16 + 16 * half)
                settle()
                for t in range(T):
                    pool.dma_start(YP[t], y_d[l][2 * t * P:2 * (t + 1) * P, :]
                                   .rearrange("(p k) n -> p k n", k=2)).then_inc(sem(f"yl{t}"), 16)
                if l == 0:
                    router_weights(1)
                    pool.wait_ge(sem("comb"), T)
                    gate_row(1, 5)

            layer(0)
            layer(1)


N_IN = 19

_INS = ["x", "c", "positions", "ada_w", "ada_b", "norm_mix", "norm_ffn", "da_w_qkv", "da_q_norm", "da_k_norm",
        "da_lambda_q1", "da_lambda_k1", "da_lambda_q2", "da_lambda_k2", "da_subln", "da_w_o", "mla_w_in",
        "mla_q_a_norm", "mla_kv_a_norm", "mla_w_uq", "mla_w_ukv", "mla_q_nope_norm", "mla_q_pe_norm",
        "mla_k_nope_norm", "mla_k_pe_norm", "mla_w_o", "moe_w_group", "moe_b_group", "moe_w_router",
        "moe_b_router", "moe_w1", "moe_w3", "moe_w2"]


def kernel(**inputs):
    import numpy as np
    import concourse.bacc as bacc
    from concourse.bass_utils import run_bass_kernel_spmd as run

    nc = bacc.Bacc("TRN2", target_bir_lowering=False, num_devices=1)
    arrays, A = {}, {}
    for name in _INS:
        a = np.ascontiguousarray(inputs[name])
        arrays["in_" + name] = a
        A[name] = nc.dram_tensor("in_" + name, a.shape, mybir.dt.from_np(a.dtype), kind="ExternalInput").ap()
    freqs = []
    for name, dim in (("inv_da", DH), ("inv_mla", ROPE)):
        a = (10000.0 ** (-np.arange(0, dim, 2, dtype=np.float64) / dim)).astype(np.float32)
        arrays[name] = a
        freqs.append(nc.dram_tensor(name, a.shape, F32, kind="ExternalInput").ap())
    out = nc.dram_tensor("out", [S, D], F32, kind="ExternalOutput").ap()
    build(nc, A, freqs[0], freqs[1], out)
    r = run(nc, [arrays], core_ids=[0])
    return r.results[0]["out"].reshape(1, S, D)
```

```python
import math
from contextlib import ExitStack

import concourse.bass as bass
from concourse import mybir

F32 = mybir.dt.float32
I32 = mybir.dt.int32
ALU = mybir.AluOpType
ACT = mybir.ActivationFunctionType
AX = mybir.AxisListType

P = 128
D = 1024
S = 512
T = S // P
C = D // P
EPS = 1e-6
NEG = -1e30

DH = 64
DA_H = 8
LAMBDA_INIT = 0.8 - 0.6 * math.exp(0.0)
NOPE, ROPE, VD = 64, 32, 64
QK = NOPE + ROPE
MLA_H = 16
QR, KVR = 384, 256
QRC, KVC = QR // P, KVR // P

G, EPG, E, FF = 4, 8, 32, 256
CAP = 64
PAIRS = E // 2
OVER = 2 * CAP
LEVELS = -(-(S - CAP) // OVER)
TAILS = 2 * S // CAP
NPAIR = PAIRS + TAILS
NOWHERE = 1 << 20
NR = G + E

UNIT = 2048
AHEAD = 8
RING = 6
NH = 512

MOD_VECTORS = ((0, 1), (1,), (0,))

MLA_PARTS = (("project", 0, 3 * T), ("attend", 0, 8), ("project", 3 * T, 4 * T), ("attend", 8, 32))

MAGIC = 1.5 * 2.0 ** 23
TWO_PI = 2 * math.pi
PI_A = 6.28125
PI_B = 0.0019350051879882812
PI_C = TWO_PI - PI_A - PI_B


class Chain:

    def __init__(self, eng, sem):
        self.eng, self.sem, self.n = eng, sem, 0

    def link(self, instruction):
        self.n += 1
        instruction.then_inc(self.sem, 1)
        self.eng.wait_ge(self.sem, self.n)


def overflow_steps(eng, tails, body):
    with eng.If(0 < tails):
        body(0, 0)
        with eng.If(1 < tails):
            body(0, 1)
            with eng.If(2 < tails):
                with eng.Fori(1, TAILS // 2) as i:
                    for b in range(2):
                        with eng.If(2 * i + b < tails):
                            body(i, b)


def wait(eng, sem, value):
    if isinstance(value, int) and value <= 0:
        return
    eng.wait_ge(sem, value)


def ada_after(n):
    before = AHEAD + sum(2 if m % 3 < 2 else 1 for m in range(n))
    return range(before, before + (2 if n % 3 < 2 else 1))


def ring_plan(A):
    ada = [A["ada_w"][l].rearrange("(p c) n -> p c n", c=C) for l in range(2)]
    qkv = A["da_w_qkv"][0].rearrange("(p c) n -> p c n", c=C)

    def ada_unit(u, slot):
        l, g, c = u // 24, u // 8 % 3, u % 8
        return ("ada", u), ada[l][:, c:c + 1, g * UNIT:(g + 1) * UNIT], 1, slot, ("ada", u + 1)

    def qkv_units(x):
        n = (x % 3) * D + (x // 3) * NH
        return [(("qkv", x, half), qkv[:, 4 * half:4 * half + 4, n:n + NH], 4, 2 * ((x + 1) % 2) + half,
                 ("da_mm", 4 * x + 4)) for half in range(2)]

    first = [ada_unit(u, u % RING) for u in range(AHEAD)] + qkv_units(0)
    for n in range(24):
        if n % 4 == 1 and n < 20:
            first += qkv_units(n // 4 + 1)
        first += [ada_unit(u, 4 + u % 2) for u in ada_after(n)]
    wo = A["da_w_o"][0].rearrange("(k p) n -> p k n", p=P)
    first += [(("wo", u), wo[:, 2 * u:2 * u + 2, :], 2, 2 + u, ("wo", 2 * T)) for u in range(4)]
    w_in = A["mla_w_in"][0].rearrange("(p c) n -> p c n", c=C)
    second = [(("in", c0 // 3), w_in[:, c0:c1, :], c1 - c0, ("lat", 2 * T)) for c0, c1 in ((0, 3), (3, 6), (6, 8))]
    uq = A["mla_w_uq"][0].rearrange("(k p) n -> p k n", p=P)
    second += [(("uq", k), uq[:, k:k + 1, :], 1, ("mla_kv", 4 * T)) for k in range(QRC)]
    ukv = A["mla_w_ukv"][0].rearrange("(k p) n -> p k n", p=P)
    second += [(("ukv", k), ukv[:, k:k + 1, :], 1, ("mla_kv", 4 * T)) for k in range(KVC)]
    wo = A["mla_w_o"][0].rearrange("(k p) n -> p k n", p=P)
    second += [(("wo", u), wo[:, 2 * u:2 * u + 2, :], 2, ("wo", 4 * T)) for u in range(4)]
    return first, [(key, src, k, n % RING, free) for n, (key, src, k, free) in enumerate(second)]


def build(nc, A, inv_da, inv_mla, out):
    stack = ExitStack()
    with stack:
        enter = stack.enter_context

        def sb(name, shape, dt=F32):
            return enter(nc.sbuf_tensor(name, shape, dt))

        sems = {}

        def sem(name):
            if name not in sems:
                sems[name] = enter(nc.semaphore("s_" + name))
            return sems[name]

        mod_d = nc.dram_tensor("mod_d", [2, 6 * D], F32)
        xn_d = [nc.dram_tensor(f"xn_d{l}", [S, D], F32) for l in range(2)]
        y_d = [nc.dram_tensor(f"y_d{l}", [2 * S, D], F32) for l in range(2)]

        ring = sb("ring", [P, RING, UNIT])
        X = sb("X", [P, T, D])
        RA = sb("RA", [P, 4096])
        RH = sb("RH", [P, 4096])
        RV = sb("RV", [P, 4096])
        RQK = sb("RQK", [P, RING * UNIT])
        SCR = sb("SCR", [P, 4096])
        PS = sb("PS", [P, 3072])
        GM = sb("GM", [P, D])
        GF = sb("GF", [P, D])
        MR = sb("MR", [P, NH])
        ident = sb("ident", [P, P])
        tri = sb("tri", [P, P])
        ones = sb("ones", [P, P])
        mneg = sb("mneg", [P, P])
        WGR = sb("WGR", [P, C, NR])
        RT = sb("RT", [P, T, 4, ROPE])
        small = sb("small", [P, 1088])
        idx = sb("idx", [P, 2, NPAIR], I32)
        ci = sb("ci", [P, 4], I32)
        CTL = sb("CTL", [1, 1 + TAILS], I32)
        posi = sb("posi", [P, T], I32)

        bump = [0]

        def sm(*shape):
            n = math.prod(shape)
            v = small[:, bump[0]:bump[0] + n]
            bump[0] += n
            assert bump[0] <= 1088
            if len(shape) == 2:
                return v.rearrange("p (a b) -> p a b", a=shape[0])
            if len(shape) == 3:
                return v.rearrange("p (a b c) -> p a b c", a=shape[0], b=shape[1])
            return v

        MODC = sm(2, 4, C)
        NRM = sm(2, 2, C)
        GC = sm(4, C)
        cc = sm(C)
        condr = sm(C, 32)
        eps = sm(1)
        ss = sm(8)
        sd = sm(8)
        rs = sm(8)
        hss = sm(2, 32)
        hsd = sm(2, 32)
        hrs = sm(2, 32)
        mx, nmx, ls, rl = sm(2, 2), sm(2, 2), sm(2, 2), sm(2, 2)
        lamv = sm(4, DH)
        lam = sm(4)
        subc = sm(1)
        qnc, knc = sm(1), sm(1)
        qan, kvan = sm(QRC), sm(KVC)
        posf = sm(T)
        invs = sm(DH // 2 + ROPE // 2)
        Wt = sm(T, 2)
        th = sm(LEVELS)
        i8 = sm(EPG)
        i32f = sm(E)
        i16f = sm(TAILS)
        bgr = sm(NR)
        gnb = SCR[:, 1024:1024 + 2 * DH + 2 * ROPE]

        def view(region, at, *shape):
            v = region[:, at:at + math.prod(shape)]
            if len(shape) == 2:
                return v.rearrange("p (a b) -> p a b", a=shape[0])
            if len(shape) == 3:
                return v.rearrange("p (a b c) -> p a b c", a=shape[0], b=shape[1])
            if len(shape) == 4:
                return v.rearrange("p (a b c d) -> p a b c d", a=shape[0], b=shape[1], c=shape[2])
            return v

        XN = view(RV, 0, T, D)
        HT = view(RH, 0, C, S)
        OTOK = view(RH, 0, T, D)
        OT = view(RA, 0, C, S)
        V = view(RV, 0, T, D)
        daq = view(RQK, 0, DA_H, S)
        dak = [view(RQK, 4096 * (1 + c), DA_H, S) for c in range(2)]
        mq = [view(RQK, 4096 * b, 4, S) for b in range(3)]
        mk = [view(RQK, 4096 * b + 2048, 4, S) for b in range(3)]
        CT = view(RA, 0, QRC + KVC, S)
        pr = [view(SCR, 1024 * b, 2, S) for b in range(2)]
        aT = [view(SCR, 2048 + 1024 * b, 2, S) for b in range(2)]
        DT = view(SCR, 0, T, 4, DH)
        SQ, M1, M2, YT = (view(PS, NH * n, NH) for n in range(4))
        LT_ = view(PS, 0, QR + KVR)
        KP = view(PS, 2560, T, ROPE)
        QY = [view(PS, 1024, 4, QK), view(SCR, 0, 4, QK)]
        KY = [view(PS, 1024 + 4 * QK, 4, QK), view(SCR, 4 * QK, 4, QK)]
        xg = [view(RV, 1024 * b, D) for b in range(2)]
        xgT = [view(RV, 2048 + 1024 * b, C, P) for b in range(2)]
        ysb = [view(PS, 1024 * b, D) for b in range(2)]
        sil = view(PS, 2048, FF)
        hid = view(PS, 2048 + FF, 2, P)
        hidT = view(PS, 2048 + 2 * FF, 2, P)
        MS = view(SCR, 3840, T + 1, E)
        iota_p = view(PS, 2048, P)
        starts = view(PS, 2048 + P, NPAIR)
        steps1 = view(PS, 2048 + P + NPAIR, NPAIR)
        pair1 = view(PS, 2048 + P + 2 * NPAIR, T, 2)
        hotp = view(SCR, 2816, 2 * T, P)
        hotn = view(SCR, 2560, 2 * T, NPAIR)
        YP = [view(RH, 0, 2, D), view(RH, 2048, 2, D), view(RA, 0, 2, D), view(RA, 2048, 2, D)]
        first_units = [region[:, at:at + UNIT] for region in (RA, RH, SCR) for at in (0, UNIT)]
        bank = [ring, RQK[:, :].rearrange("p (s n) -> p s n", s=RING)]

        PB = [enter(nc.psum_tensor(f"PB{n}", [P, NH], F32)) for n in range(8)]

        streams = ring_plan(A)
        plan, arrival, fills, holder = [], [{}, {}], [0] * (2 * RING), [None] * RING
        first_slot, moe_fills, moe_holder = [], [], []
        for l in range(2):
            now = []
            for key, src, k, slot, free in streams[l]:
                fills[slot] += 1
                now.append((src, k, slot, holder[slot]))
                arrival[l][key] = (slot, 16 * fills[slot])
                holder[slot] = free
            plan.append(now)
            first_slot.append((slot + 1) % RING)
            moe_fills.append(list(fills))
            moe_holder.append(list(holder))
            for s in range(2 * RING):
                fills[s] += PAIRS // 2 - 1 if s < RING else PAIRS // 2
            holder = [(f"y{l}", PAIRS - 1)] * RING
        s_w = [sem(f"w{s}") for s in range(2 * RING)]

        w1 = [A["moe_w1"][l].rearrange("g e (p c) f -> (g e) p (c f)", c=C) for l in range(2)]
        w3 = [A["moe_w3"][l].rearrange("g e (p c) f -> (g e) p (c f)", c=C) for l in range(2)]
        w2 = [A["moe_w2"][l].rearrange("g e (p c) d -> (g e) p (c d)", c=FF // P) for l in range(2)]

        def slots(l):
            return [(first_slot[l] + k) % RING for k in range(6)]

        block = enter(nc.Block())

        @block.sync
        def _(sp):
            def stream(l):
                for n, (src, k, slot, held) in enumerate(plan[l]):
                    if l == 1 and n == 3:
                        sp.wait_ge(sem("yl3"), 16)
                    if held:
                        sp.wait_ge(sem(held[0]), held[1])
                    cols = src.shape[-1]
                    dst = ring[:, slot, 0:k * cols].rearrange("p (k n) -> p k n", k=k)
                    sp.dma_start(dst, src).then_inc(s_w[slot], 16)

            def experts(l, dst, free, e0, e1, arrive):
                for k, (w, e) in enumerate(((w1, e0), (w1, e1), (w3, e0), (w3, e1), (w2, e0), (w2, e1))):
                    free(k)
                    src = w[l][bass.ds(e, 1)].rearrange("a p n -> p (a n)")
                    sp.dma_start(dst(k), src).then_inc(arrive(k), 16)

            def main(l, wb, e0, free):
                experts(l, lambda k: bank[wb][:, slots(l)[k], :], free, e0, e0 + 1, lambda k: s_w[RING * wb + slots(l)[k]])

            def free_first(l):
                def free(k):
                    if k < 2:
                        sp.wait_ge(sem("wo"), 2 * T * (l + 1))
                    elif k < 4:
                        sp.wait_ge(sem("lg"), T * (l + 1))
                    else:
                        sp.wait_ge(sem("ctl"), l + 1)
                return free

            def free_ring(l):
                def free(k):
                    name, value = moe_holder[l][slots(l)[k]]
                    sp.wait_ge(sem(name), value)
                return free

            def free_later(l, n):
                return lambda k: sp.wait_ge(sem(f"{'aby'[k // 2]}{l}"), n - 1)

            for l in range(2):
                stream(l)
                main(l, 1, 2, lambda k: sp.wait_ge(sem("sc"), 32 * (l + 1)))
                main(l, 0, 4, free_ring(l))
                experts(l, lambda k: first_units[k], free_first(l), 0, 1, lambda k: sem(f"wx{k // 2}"))
                with sp.Fori(1, PAIRS // 2 - 1) as i:
                    main(l, 1, 4 * i + 2, free_later(l, 2 * i + 1))
                    main(l, 0, 4 * i + 4, free_later(l, 2 * i + 2))
                main(l, 1, 2 * PAIRS - 2, free_later(l, PAIRS - 1))
                sp.wait_ge(sem("ctl"), l + 1)
                tails = sp.value_load(CTL[0:1, 0:1], min_val=0, max_val=TAILS)

                def overflow(i, b):
                    e = sp.value_load(CTL[0:1, bass.ds(2 * i + b + 1, 1)], min_val=0, max_val=E - 1)
                    for m, (w, done) in enumerate(((w1, "a"), (w3, "b"), (w2, "y"))):
                        sp.wait_ge(sem(f"{done}{l}"), PAIRS + 2 * i + b - 1)
                        sp.dma_start(bank[b][:, slots(l)[2 * m], :],
                                     w[l][bass.ds(e, 1)].rearrange("a p n -> p (a n)")).then_inc(sem(f"wt{l}{b}"), 16)
                overflow_steps(sp, tails, overflow)
                if l == 0:
                    with sp.If(0 < tails):
                        sp.wait_ge(sem("y0"), tails + PAIRS)
                        sp.sem_inc(sem("sp_turns"), 1)
            for t in range(T):
                sp.wait_ge(sem("comb"), T + t + 1)
                sp.dma_start(out[t * P:(t + 1) * P, :], X[:, t, :]).then_inc(sem("out"), 16)
            sp.wait_ge(sem("out"), 16 * T)

        @block.tensor
        def _(pe):
            mm = nc.tensor.matmul

            def take(l, *key):
                slot, value = arrival[l][key]
                pe.wait_ge(s_w[slot], value)
                return ring[:, slot, :]

            def ada(u):
                w = take(0, "ada", u)
                a, c = divmod(u, C)
                if c == 0:
                    if a > 1:
                        columns(a - 1)
                    wait(pe, sem("mr"), a - 1)
                for j in range(4):
                    last = mm(PB[7 - 2 * (a % 2)][32 * j:32 * j + 32, :], condr[:, c, :], w[:, j * NH:(j + 1) * NH],
                              start=c == 0, stop=c == C - 1)
                last.then_inc(sem("ada"), 1)

            def columns(a):
                pe.wait_ge(sem("mr"), a + 1)
                wait(pe, sem("mc"), a)
                for v in MOD_VECTORS[a % 3]:
                    for c in range(C):
                        for j in range(2):
                            last = mm(PB[6][64 * j:64 * j + 64, v * C + c:v * C + c + 1], MR[:, c:NH:C],
                                      ident[:, 64 * v + 32 * j:64 * v + 32 * j + 1], start=True, stop=True)
                last.then_inc(sem("mcp"), 1)

            def transpose_x(k, t):
                if k in (1, 3):
                    pe.wait_ge(sem("oev"), 8 * (k // 2) + 2 * t + 2)
                pe.wait_ge(sem("xn"), 4 * k + t + 1)
                for c in range(C):
                    last = nc.tensor.transpose(PB[2 * t + c // 4][:, c % 4 * P:(c % 4 + 1) * P], XN[:, t, c * P:(c + 1) * P],
                                               ident[:, :])
                last.then_inc(sem("xt"), 1)

            def modulated(k, t):
                pe.wait_ge(sem("hA"), 4 * k + t + 1)
                pe.wait_ge(sem("hD"), 4 * k + t + 1)

            def da_project():
                def turn(n):
                    m = (n // 12) * 8 + n % 12
                    wait(pe, sem("datev"), m)
                    pe.wait_ge(sem("day"), m + 1)
                    for h in range(4):
                        last = nc.tensor.transpose(PB[4][:, h * P:(h + 1) * P], YT[:, h * P:(h + 1) * P], ident[:, :])
                    last.then_inc(sem("dat"), 1)

                for hb in range(2):
                    for w in range(3):
                        us = [take(0, "qkv", 3 * hb + w, half) for half in range(2)]
                        for t in range(T):
                            n = hb * 12 + w * 4 + t
                            if n < T:
                                modulated(0, t)
                            wait(pe, sem("daev"), n - 3)
                            for c in range(C):
                                last = mm(PB[n % 4][:, :], HT[:, c, t * P:(t + 1) * P],
                                          us[c // 4][:, (c % 4) * NH:(c % 4 + 1) * NH], start=c == 0, stop=c == C - 1)
                            last.then_inc(sem("da_mm"), 1)
                            if 0 < n and (n - 1) % 12 < 8:
                                turn(n - 1)
                            if n == 0:
                                modulated(0, T - 1)
                            for u in ada_after(n):
                                ada(u)

            def scores(l, i, pair):
                g, t = divmod(i, T)
                L = (t + 1) * P
                for a in range(2):
                    o = PB[2 * pair + a]
                    if l == 0:
                        mm(o[:, 0:L], daq[:, g, t * P:L], dak[a][:, g, 0:L], start=True, stop=False)
                    else:
                        h = 2 * (g % 2) + a
                        mm(o[:, 0:L], mq[g // 2 % 3][0:QK, h, t * P:L], mk[g // 2 % 3][0:QK, h, 0:L],
                           start=True, stop=False)
                    last = mm(o[:, t * P:L], ident[:, :], mneg[:, :], start=False, stop=True)
                last.then_inc(sem("sc"), 1)

            def turn_probabilities(l, i):
                t, b, n = i % T, i % 2, 32 * l + i
                pe.wait_ge(sem("exp" if l else "p"), n + 1)
                wait(pe, sem("tev"), n)
                if l == 1:
                    wait(pe, sem("tev1"), i)
                for a in range(1 + l):
                    for k in range(t + 1):
                        last = nc.tensor.transpose(PB[4 + a][:, k * P:(k + 1) * P], pr[b][:, a, k * P:(k + 1) * P], ident[:, :])
                last.then_inc(sem("tr"), 1)

            def values(l, i):
                (g, t), b, n = divmod(i, T), i % 2, 32 * l + i
                pe.wait_ge(sem("tev"), n + 1)
                if l == 1:
                    pe.wait_ge(sem("tev1"), i + 1)
                wait(pe, sem("oe"), n - 1)
                if l == 0:
                    for k in range(t + 1):
                        last = mm(PB[6 + b][:, 0:P], aT[b][:, 0, k * P:(k + 1) * P], V[:, k, g * P:(g + 1) * P],
                                  start=k == 0, stop=k == t)
                else:
                    for a in range(2):
                        h = 2 * g + a
                        for k in range(t + 1):
                            last = mm(PB[6 + b][:, a * VD:(a + 1) * VD], aT[b][:, a, k * P:(k + 1) * P],
                                      V[:, k, h * VD:(h + 1) * VD], start=k == 0, stop=k == t)
                last.then_inc(sem("av"), 1)

            def da_attention():
                scores(0, 0, 0)
                scores(0, 1, 1)
                for i in range(32):
                    if i + 2 < 32:
                        pe.wait_ge(sem("exp"), i + 1)
                        scores(0, i + 2, i % 2)
                    if i > 0:
                        values(0, i - 1)
                    turn_probabilities(0, i)
                values(0, 31)

            def project_out(l):
                k1 = 2 * l + 1

                def turn(t):
                    if l == 0:
                        pe.wait_ge(sem("on"), t + 1)
                    else:
                        pe.wait_ge(sem("oe"), 64)
                    for k in range(C):
                        last = nc.tensor.transpose(PB[2 * t + k // 4][:, k % 4 * P:(k % 4 + 1) * P], OTOK[:, t, k * P:(k + 1) * P],
                                                   ident[:, :])
                    last.then_inc(sem("ott"), 1)

                def product(t):
                    pe.wait_ge(sem("otev"), 4 * l + t + 1)
                    for n in range(2):
                        for k in range(C):
                            last = mm(PB[2 * t + n][:, :], OT[:, k, t * P:(t + 1) * P],
                                      us[k // 2][:, (k % 2) * D + n * NH:(k % 2) * D + (n + 1) * NH],
                                      start=k == 0, stop=k == C - 1)
                        last.then_inc(sem("wo"), 1)

                def logits(t):
                    modulated(k1, t)
                    for c in range(C):
                        last = mm(PB[0][:, t * NR:(t + 1) * NR], HT[:, c, t * P:(t + 1) * P], WGR[:, c, :],
                                  start=c == 0, stop=c == C - 1)
                    last.then_inc(sem("lg"), 1)

                turn(0)
                turn(1)
                us = [take(l, "wo", u) for u in range(4)]
                product(0)
                turn(2)
                turn(3)
                product(1)
                transpose_x(k1, 0)
                product(2)
                transpose_x(k1, 1)
                pe.wait_ge(sem("wgr"), 32 * (l + 1))
                logits(0)
                product(3)
                transpose_x(k1, 2)
                logits(1)
                transpose_x(k1, 3)
                logits(2)
                logits(3)

            def route(l):
                pe.wait_ge(sem("M"), l + 1)
                M = SCR[:, 256:256 + T * E]
                mm(PB[1][:, 0:T * E], tri[:, :], M, start=True, stop=False)
                mm(PB[1][:, 0:T * E], ones[:, :], MS[:, 0:T], start=False, stop=True)
                mm(PB[1][:, T * E:(T + 1) * E], ones[:, :], MS[:, T], start=True, stop=True).then_inc(sem("rank"), 1)
                pe.wait_ge(sem("hot"), l + 1)
                for j in range(2 * T):
                    last = mm(PB[2][:, 0:NPAIR], hotp[:, j], hotn[:, j], start=j == 0, stop=j == 2 * T - 1)
                last.then_inc(sem("tab"), 1)

            def turn_rows(l, b, q, n):
                pe.wait_ge(sem(f"gath{l}{b}"), 16 * (q + 1))
                wait(pe, sem(f"xA{l}"), n)
                wait(pe, sem(f"xD{l}"), n)
                for c in range(C):
                    last = nc.tensor.transpose(PB[c % 2][:, (c // 2) * P:(c // 2 + 1) * P], xg[b][:, c * P:(c + 1) * P], ident[:, :])
                last.then_inc(sem(f"xt{l}"), 1)

            def expert_step(l, b, n, units, arrived, tiles, turn_next=lambda: None):
                arrived(0)
                pe.wait_ge(sem(f"xA{l}"), n + 1)
                pe.wait_ge(sem(f"xD{l}"), n + 1)
                for m, (o, done, read) in enumerate(((PB[2], "a", "sil"), (PB[3], "b", "hid"))):
                    if m:
                        arrived(1)
                    wait(pe, sem(f"{read}{l}"), n)
                    for c in range(C):
                        for s0, s1, e in tiles:
                            last = mm(o[s0:s1, 0:FF], xgT[b][:, c, s0:s1],
                                      units(2 * m + e)[:, c * FF:(c + 1) * FF], start=c == 0, stop=c == C - 1)
                    last.then_inc(sem(f"{done}{l}"), 1)
                turn_next()
                pe.wait_ge(sem(f"hid{l}"), n + 1)
                wait(pe, sem(f"hT{l}"), n)
                for c in range(2):
                    last = nc.tensor.transpose(PB[4][:, c * P:(c + 1) * P], hid[:, c, :], ident[:, :])
                last.then_inc(sem(f"ht{l}"), 1)
                arrived(2)
                pe.wait_ge(sem(f"hT{l}"), n + 1)
                wait(pe, sem(f"yD{l}"), n)
                for m in range(2):
                    for c in range(2):
                        for s0, s1, e in tiles:
                            last = mm(PB[5 + m][s0:s1, :], hidT[:, c, s0:s1],
                                      units(4 + e)[:, c * D + m * NH:c * D + (m + 1) * NH], start=c == 0, stop=c == 1)
                last.then_inc(sem(f"y{l}"), 1)

            def experts(l):
                pair = ((0, CAP, 0), (CAP, 2 * CAP, 1))

                def stored(b):
                    return lambda k: bank[b][:, slots(l)[k], :]

                def step(i, b, turn_next=lambda: None):
                    def arrived(m):
                        for e in range(2):
                            s = RING * b + slots(l)[2 * m + e]
                            pe.wait_ge(s_w[s], 16 * (moe_fills[l][s] + b) + 16 * i)
                    expert_step(l, b, 2 * i + b, stored(b), arrived, pair, turn_next)
                turn_rows(l, 0, 0, 0)
                expert_step(l, 0, 0, lambda k: first_units[k], lambda m: pe.wait_ge(sem(f"wx{m}"), 32 * (l + 1)), pair,
                            lambda: turn_rows(l, 1, 0, 1))
                step(0, 1, lambda: turn_rows(l, 0, 1, 2))
                with pe.Fori(1, PAIRS // 2 - 1) as i:
                    step(i, 0, lambda: turn_rows(l, 1, i, 2 * i + 1))
                    step(i, 1, lambda: turn_rows(l, 0, i + 1, 2 * i + 2))
                step(PAIRS // 2 - 1, 0, lambda: turn_rows(l, 1, PAIRS // 2 - 1, PAIRS - 1))
                step(PAIRS // 2 - 1, 1)
                pe.wait_ge(sem("ctl"), l + 1)
                tails = pe.value_load(CTL[0:1, 0:1], min_val=0, max_val=TAILS)

                def overflow(i, b):
                    pe.wait_ge(sem(f"wt{l}{b}"), 48 * i + 48)
                    turn_rows(l, b, PAIRS // 2 + i, PAIRS + 2 * i + b)
                    expert_step(l, b, PAIRS + 2 * i + b, stored(b), lambda m: None, ((0, OVER, 0),))
                overflow_steps(pe, tails, overflow)

            def latents():
                W = QR + KVR + ROPE

                def turn(t):
                    pe.wait_ge(sem("ln"), t + 1)
                    wait(pe, sem("ltevA"), t)
                    wait(pe, sem("ltevD"), t)
                    for k in range(QRC + KVC):
                        o = PB[4][:, k * P:(k + 1) * P] if k < QRC else PB[5][:, (k - QRC) * P:(k - QRC + 1) * P]
                        last = nc.tensor.transpose(o, LT_[:, k * P:(k + 1) * P], ident[:, :])
                    last.then_inc(sem("ltt"), 1)

                def project(t):
                    wait(pe, sem("lev"), t - 1)
                    modulated(2, t)
                    for m, (c0, c1) in enumerate(((0, QR), (QR, W))):
                        for c in range(C):
                            last = mm(PB[2 * (t % 2) + m][:, 0:c1 - c0], HT[:, c, t * P:(t + 1) * P],
                                      us[c // 3][:, (c % 3) * W + c0:(c % 3) * W + c1], start=c == 0, stop=c == C - 1)
                        last.then_inc(sem("lat"), 1)

                transpose_x(2, 0)
                transpose_x(2, 1)
                us = [take(1, "in", u) for u in range(3)]
                project(0)
                transpose_x(2, 2)
                project(1)
                transpose_x(2, 3)
                modulated(2, 3)
                turn(0)
                for t in range(2, T):
                    project(t)
                    turn(t - 1)
                turn(T - 1)

            def mla():
                uq = [take(1, "uq", k) for k in range(QRC)]
                ukv = [take(1, "ukv", k) for k in range(KVC)]

                def project(n):
                    (hb, t), pair = divmod(n, T), n % 2
                    wait(pe, sem("mev"), n - 1)
                    for k in range(QRC):
                        last = mm(PB[2 * pair][:, 0:4 * QK], CT[:, k, t * P:(t + 1) * P],
                                  uq[k][:, hb * 4 * QK:(hb + 1) * 4 * QK], start=k == 0, stop=k == QRC - 1)
                    last.then_inc(sem("mla_q"), 1)
                    for k in range(KVC):
                        last = mm(PB[2 * pair + 1][:, :], CT[:, QRC + k, t * P:(t + 1) * P],
                                  ukv[k][:, hb * NH:(hb + 1) * NH], start=k == 0, stop=k == KVC - 1)
                    last.then_inc(sem("mla_kv"), 1)

                def turn_qk(n):
                    pe.wait_ge(sem("my"), n + 1)
                    wait(pe, sem("mtev"), n)
                    wait(pe, sem("mtevD"), n)
                    for m, y in enumerate((QY, KY)):
                        for h in range(4):
                            last = nc.tensor.transpose(PB[4 + m][0:QK, h * P:(h + 1) * P], y[n % 2][:, h, :], ident[:, :])
                    last.then_inc(sem("mt"), 1)

                def project_part(n0, n1):
                    attended = MLA_PARTS[1][2] if n0 else 0
                    if attended:
                        pe.wait_ge(sem("exp"), 32 + attended)
                        pe.wait_ge(sem("tev"), 32 + attended)
                        pe.wait_ge(sem("tev1"), attended)
                    for n in range(n0, n1):
                        project(n)
                        if n >= n0 + 2:
                            turn_qk(n - 2)
                    turn_qk(n1 - 2)
                    turn_qk(n1 - 1)
                    for name in ("mtev", "mtevD", "msq", "mev"):
                        pe.wait_ge(sem(name), n1)

                def attention_part(i0, i1):
                    scores(1, i0, 0)
                    scores(1, i0 + 1, 1)
                    for i in range(i0, i1):
                        if i + 2 < i1:
                            pe.wait_ge(sem("exp"), 32 + i + 1)
                            scores(1, i + 2, i % 2)
                        turn_probabilities(1, i)
                        if i > i0:
                            values(1, i - 1)
                    values(1, i1 - 1)

                pe.wait_ge(sem("ltevA"), T)
                pe.wait_ge(sem("ltevD"), T)
                for part, first, end in MLA_PARTS:
                    (project_part if part == "project" else attention_part)(first, end)

            pe.wait_ge(sem("const"), 3)
            pe.wait_ge(sem("cond"), 1)
            for u in range(AHEAD):
                ada(u)
                if u >= AHEAD - 3:
                    transpose_x(0, u - (AHEAD - 3))
            columns(0)
            pe.wait_ge(sem("mc"), 1)
            transpose_x(0, 3)
            da_project()
            columns(5)
            pe.wait_ge(sem("mc"), 6)
            pe.wait_ge(sem("datev"), 16)
            pe.wait_ge(sem("daev"), 24)
            pe.wait_ge(sem("pool"), 5)
            da_attention()
            pe.wait_ge(sem("oe"), 32)
            project_out(0)
            route(0)
            experts(0)
            latents()
            mla()
            project_out(1)
            route(1)
            experts(1)

        @block.scalar
        def _(act):
            fn = nc.scalar.activation
            chain = Chain(act, sem("act"))

            def bc(v, n=P):
                return v.partition_broadcast(n)

            loads = [
                (posi[:, :], A["positions"][0].rearrange("(t p) -> p t", p=P)),
                (NRM[:, 0], A["norm_mix"].rearrange("l (p c) -> p l c", c=C)),
                (NRM[:, 1], A["norm_ffn"].rearrange("l (p c) -> p l c", c=C)),
                (gnb[:, 0:DH], bc(A["da_q_norm"][0])),
                (gnb[:, DH:2 * DH], bc(A["da_k_norm"][0])),
                (gnb[:, 2 * DH:2 * DH + ROPE], bc(A["mla_q_pe_norm"][0])),
                (gnb[:, 2 * DH + ROPE:], bc(A["mla_k_pe_norm"][0])),
                (lamv[:, 0], bc(A["da_lambda_q1"][0])),
                (lamv[:, 1], bc(A["da_lambda_k1"][0])),
                (lamv[:, 2], bc(A["da_lambda_q2"][0])),
                (lamv[:, 3], bc(A["da_lambda_k2"][0])),
                (subc, A["da_subln"][0].rearrange("(p c) -> p c", c=1)),
                (qnc[0:NOPE, :], A["mla_q_nope_norm"][0].rearrange("(p c) -> p c", c=1)),
                (knc[0:NOPE, :], A["mla_k_nope_norm"][0].rearrange("(p c) -> p c", c=1)),
                (qan, A["mla_q_a_norm"][0].rearrange("(k p) -> p k", p=P)),
                (kvan, A["mla_kv_a_norm"][0].rearrange("(k p) -> p k", p=P)),
                (invs[:, 0:DH // 2], bc(inv_da)),
                (invs[:, DH // 2:], bc(inv_mla)),
            ]
            with nc.allow_non_contiguous_dma(reason="short vectors"):
                act.dma_start(cc, A["c"][0].rearrange("(p c) -> p c", c=C)).then_inc(sem("c"), 16)
            for t in range(T):
                act.dma_start(X[:, t, :], A["x"][0, t * P:(t + 1) * P, :]).then_inc(sem("x"), 16)
            act.wait_ge(sem("c"), 16)
            fn(cc, cc, ACT.Silu).then_inc(sem("silc"), 1)
            for dst, src in loads:
                with nc.allow_non_contiguous_dma(reason="short vectors"):
                    act.dma_start(dst, src).then_inc(sem("in"), 16)
            assert len(loads) == N_IN

            def squares(k, t):
                if k == 0:
                    act.wait_ge(sem("x"), 16 * T)
                elif k == 2:
                    act.wait_ge(sem("comb"), t + 1)
                else:
                    act.wait_ge(sem("res"), 4 * (k // 2) + t + 1)
                if t == 0:
                    wait(act, sem("xn"), 4 * k)
                wait(act, sem("sd"), 4 * k + t)
                fn(view(PS, 0, D), X[:, t, :], ACT.Square, accum_out=ss[:, t:t + 1]).then_inc(sem("sq"), 1)
                act.wait_ge(sem("sq"), 4 * k + t + 1)
                fn(sd[:, t:t + 1], ss[:, t:t + 1], ACT.Sqrt, bias=eps, scale=1.0 / D).then_inc(sem("sd"), 1)

            def modulate(k, t):
                l, w = divmod(k, 2)
                act.wait_ge(sem("gc"), k + 1)
                act.wait_ge(sem("xt"), 4 * k + t + 1)
                if k == 2:
                    act.wait_ge(sem("comb"), 2)
                for c in range(C // 2):
                    last = fn(HT[:, c, t * P:(t + 1) * P], PB[2 * t][:, c * P:(c + 1) * P], ACT.Identity,
                              bias=MODC[:, l, 2 * w, c:c + 1], scale=GC[:, k, c:c + 1])
                last.then_inc(sem("hA"), 1)

            def norm(k):
                squares(k, 0)
                for t in range(T):
                    if t + 1 < T:
                        squares(k, t + 1)
                    modulate(k, t)

            def root(out_, in_, scale, s):
                fn(out_, in_, ACT.Sqrt, bias=eps, scale=scale).then_inc(sem(s), 1)

            def da_project():
                def turned(m):
                    n = (m // 8) * 12 + m % 8
                    hb, w, t = n // 12, n % 12 // 4, n % 4
                    act.wait_ge(sem("dat"), m + 1)
                    src = PB[4][:, :].rearrange("p (h q) -> p h q", h=4)
                    if w == 0:
                        fn(daq[:, 4 * hb:4 * hb + 4, t * P:(t + 1) * P], src, ACT.Identity).then_inc(sem("datev"), 1)
                    else:
                        for a in range(2):
                            last = fn(dak[a][64 * a:64 * a + 64, 4 * hb:4 * hb + 4, t * P:(t + 1) * P],
                                      src[64 * a:64 * a + 64], ACT.Identity)
                        last.then_inc(sem("datev"), 1)

                for hb in range(2):
                    for w in range(3):
                        for t in range(T):
                            n = hb * 12 + w * 4 + t
                            m = hb * 8 + w * 4 + t
                            act.wait_ge(sem("da_mm"), n + 1)
                            if w == 2:
                                act.wait_ge(sem("daev"), n)
                                fn(V[:, t, hb * NH:(hb + 1) * NH], PB[n % 4][:, :], ACT.Identity).then_inc(sem("daev"), 1)
                            else:
                                wait(act, sem("dss"), m)
                                fn(SQ, PB[n % 4][:, :], ACT.Square).then_inc(sem("dsq"), 1)
                                act.wait_ge(sem("dss"), m + 1)
                                wait(act, sem("drs"), m - 1)
                                root(hsd[:, m % 2, 0:8], hss[:, m % 2, 0:8], 1.0 / DH, "dsd")
                            if 0 < n and (n - 1) % 12 < 8:
                                turned((n - 1) // 12 * 8 + (n - 1) % 12)

            def exps(l, i, pair):
                t, b, n = i % T, i % 2, 32 * l + i
                L = (t + 1) * P
                act.wait_ge(sem("nm"), n + 1)
                wait(act, sem("tr"), n - 1)
                wait(act, sem("p"), n - 1)
                for a in range(2):
                    last = fn(pr[b][:, a, 0:L], PB[2 * pair + a][:, 0:L], ACT.Exp, bias=nmx[:, b, a:a + 1],
                              scale=(DH, QK)[l] ** -0.5, accum_out=ls[:, b, a:a + 1])
                last.then_inc(sem("exp"), 1)

            def probabilities_out(l, i):
                t, b, n = i % T, i % 2, 32 * l + i
                L = (t + 1) * P
                act.wait_ge(sem("tr"), n + 1)
                wait(act, sem("av"), n - 1)
                fn(aT[b][:, 0, 0:L], PB[4][:, 0:L], ACT.Identity).then_inc(sem("tev"), 1)

            def da_attention():
                def output(i):
                    (g, t), b = divmod(i, T), i % 2
                    act.wait_ge(sem("av"), i + 1)
                    fn(OTOK[:, t, g * P:(g + 1) * P], PB[6 + b][:, 0:P], ACT.Identity).then_inc(sem("oe"), 1)

                exps(0, 0, 0)
                exps(0, 1, 1)
                for i in range(32):
                    probabilities_out(0, i)
                    if i + 2 < 32:
                        exps(0, i + 2, i % 2)
                    if i > 0:
                        output(i - 1)
                output(31)

            def output_norm(t):
                wait(act, sem("oss"), t)
                if t == 0:
                    act.wait_ge(sem("oe"), 32)
                    act.wait_ge(sem("day"), 16)
                fn(view(PS, 0, D), OTOK[:, t, :], ACT.Square).then_inc(sem("osq"), 1)
                act.wait_ge(sem("oss"), t + 1)
                root(hsd[:, 0, 8 * t:8 * t + 8], hss[:, 0, 8 * t:8 * t + 8], 1.0 / P, "osd")

            def output_turn(l, t):
                act.wait_ge(sem("ott"), 4 * l + t + 1)
                for half in range(2):
                    dst = OT[:, 4 * half:4 * half + 4, t * P:(t + 1) * P]
                    src = PB[2 * t + half][:, :].rearrange("p (k q) -> p k q", k=4)
                    last = fn(dst, src, ACT.Identity, scale=subc if l == 0 else 1.0)
                last.then_inc(sem("otev"), 1)

            def latents():
                for t in range(T):
                    o = [PB[2 * (t % 2)], PB[2 * (t % 2) + 1]]
                    act.wait_ge(sem("lat"), 2 * t + 2)
                    wait(act, sem("lrs"), t)
                    sq = view(PS, 1024, QR)
                    chain.link(fn(sq, o[0][:, 0:QR], ACT.Square, accum_out=ss[:, 4:5]))
                    chain.link(fn(sq[:, 0:KVR], o[1][:, 0:KVR], ACT.Square, accum_out=ss[:, 5:6]))
                    chain.link(fn(sq[:, 0:ROPE], o[1][:, KVR:KVR + ROPE], ACT.Square, accum_out=ss[:, 6:7]))
                    fn(sd[:, 4:5], ss[:, 4:5], ACT.Sqrt, bias=eps, scale=1.0 / QR)
                    fn(sd[:, 5:6], ss[:, 5:6], ACT.Sqrt, bias=eps, scale=1.0 / KVR)
                    fn(sd[:, 6:7], ss[:, 6:7], ACT.Sqrt, bias=eps, scale=1.0 / ROPE).then_inc(sem("lsd"), 1)
                    if t:
                        turn_latents(t - 1)
                turn_latents(T - 1)

            def turn_latents(t):
                act.wait_ge(sem("ltt"), t + 1)
                for k in range(QRC):
                    last = fn(CT[:, k, t * P:(t + 1) * P], PB[4][:, k * P:(k + 1) * P], ACT.Identity, scale=qan[:, k:k + 1])
                last.then_inc(sem("ltevA"), 1)

            def mla():
                def project(n):
                    hb, t = divmod(n, T)
                    b = n % 2
                    sq = view(PS, 0, 4, QK)
                    sk = view(PS, 4 * QK, 4, NOPE)
                    kv = PB[2 * b + 1][:, :].rearrange("p (h x) -> p h x", h=4)
                    act.wait_ge(sem("mla_q"), n + 1)
                    wait(act, sem("mss"), n)
                    fn(sq, PB[2 * b][:, 0:4 * QK].rearrange("p (h x) -> p h x", h=4), ACT.Square)
                    act.wait_ge(sem("mla_kv"), n + 1)
                    fn(sk, kv[:, :, 0:NOPE], ACT.Square)
                    fn(V[:, t, hb * 256:(hb + 1) * 256].rearrange("p (h x) -> p h x", h=4), kv[:, :, NOPE:],
                       ACT.Identity).then_inc(sem("msq"), 1)
                    act.wait_ge(sem("mss"), n + 1)
                    fn(hsd[:, b, 0:8], hss[:, b, 0:8], ACT.Ln, bias=eps, scale=1.0 / NOPE)
                    fn(hsd[:, b, 8:12], hss[:, b, 8:12], ACT.Ln, bias=eps, scale=1.0 / ROPE).then_inc(sem("msd"), 1)
                    act.wait_ge(sem("msd"), n + 1)
                    wait(act, sem("my"), n - 1)
                    fn(hrs[:, b, 0:12], hsd[:, b, 0:12], ACT.Exp, scale=-0.5).then_inc(sem("mrs"), 1)

                def queries_out(n):
                    hb, t = divmod(n, T)
                    act.wait_ge(sem("mt"), n + 1)
                    wait(act, sem("sc"), 32 + 8 * max(hb - 2, 0))
                    fn(mq[hb % 3][0:QK, :, t * P:(t + 1) * P], PB[4][0:QK, :].rearrange("p (h q) -> p h q", h=4),
                       ACT.Identity, scale=qnc[0:QK, :]).then_inc(sem("mtev"), 1)

                def project_part(n0, n1):
                    for n in range(n0, n1):
                        project(n)
                        if n >= n0 + 2:
                            queries_out(n - 2)
                    queries_out(n1 - 2)
                    queries_out(n1 - 1)

                def attention_part(i0, i1):
                    exps(1, i0, 0)
                    exps(1, i0 + 1, 1)
                    for i in range(i0, i1):
                        probabilities_out(1, i)
                        if i + 2 < i1:
                            exps(1, i + 2, i % 2)

                act.preload_act_table_set("natural_log_exp_and_others")
                for part, first, end in MLA_PARTS:
                    (project_part if part == "project" else attention_part)(first, end)

            def gate(l):
                act.wait_ge(sem("gl"), l + 1)
                v = view(SCR, 0, T, G)
                fn(v, v, ACT.Exp).then_inc(sem("gle"), 1)
                act.wait_ge(sem("el"), l + 1)
                v = view(SCR, 512, T, EPG)
                fn(v, v, ACT.Exp).then_inc(sem("ele"), 1)

            def modulate_rows(l, b, n, before):
                act.wait_ge(sem(f"xt{l}"), n + 1)
                wait(act, sem(f"b{l}"), before)
                for c in range(0, C, 2):
                    last = fn(xgT[b][:, c, :], PB[0][:, (c // 2) * P:(c // 2 + 1) * P], ACT.Identity,
                              bias=MODC[:, l, 2, c:c + 1], scale=GC[:, 2 * l + 1, c:c + 1])
                last.then_inc(sem(f"xA{l}"), 1)

            def expert_step(l, n):
                act.wait_ge(sem(f"a{l}"), n + 1)
                wait(act, sem(f"hid{l}"), n)
                fn(sil, PB[2][:, 0:FF], ACT.Silu).then_inc(sem(f"sil{l}"), 1)
                act.wait_ge(sem(f"ht{l}"), n + 1)
                wait(act, sem(f"y{l}"), n)
                fn(hidT, PB[4][:, 0:2 * P].rearrange("p (a q) -> p a q", a=2), ACT.Identity).then_inc(sem(f"hT{l}"), 1)

            def experts(l):
                modulate_rows(l, 0, 0, 0)
                expert_step(l, 0)
                modulate_rows(l, 1, 1, 0)
                expert_step(l, 1)
                modulate_rows(l, 0, 2, 1)
                with act.Fori(1, PAIRS // 2 - 1) as i:
                    expert_step(l, 2 * i)
                    modulate_rows(l, 1, 2 * i + 1, 2 * i)
                    expert_step(l, 2 * i + 1)
                    modulate_rows(l, 0, 2 * i + 2, 2 * i + 1)
                expert_step(l, PAIRS - 2)
                modulate_rows(l, 1, PAIRS - 1, PAIRS - 2)
                expert_step(l, PAIRS - 1)
                act.wait_ge(sem("ctl"), l + 1)
                tails = act.value_load(CTL[0:1, 0:1], min_val=0, max_val=TAILS)

                def overflow(i, b):
                    modulate_rows(l, b, PAIRS + 2 * i + b, PAIRS + 2 * i + b - 1)
                    expert_step(l, PAIRS + 2 * i + b)
                overflow_steps(act, tails, overflow)

            act.wait_ge(sem("cond"), 1)
            for t in range(T):
                squares(0, t)
            for t in range(T):
                modulate(0, t)
            act.wait_ge(sem("lams"), 1)
            fn(lam[:, 0:2], lam[:, 0:2], ACT.Exp).then_inc(sem("lame"), 1)
            act.wait_ge(sem("ang"), 1)
            fn(view(SCR, 2048, T, 48), view(SCR, 1280, T, 48), ACT.Sin)
            fn(view(SCR, 2304, T, 48), view(SCR, 1280, T, 48), ACT.Sin, scale=0.5).then_inc(sem("sin"), 1)
            da_project()
            da_attention()
            output_norm(0)
            output_norm(1)
            output_turn(0, 0)
            output_norm(2)
            output_turn(0, 1)
            output_norm(3)
            output_turn(0, 2)
            output_turn(0, 3)
            norm(1)
            gate(0)
            experts(0)
            norm(2)
            latents()
            mla()
            for t in range(T):
                output_turn(1, t)
            norm(3)
            gate(1)
            experts(1)

        @block.vector
        def _(dve):
            v = nc.vector
            chain = Chain(dve, sem("dve"))
            link = chain.link
            tt, ts, stt, red = v.tensor_tensor, v.tensor_scalar, v.scalar_tensor_tensor, v.tensor_reduce

            def over(ap, axis, n):
                ap = ap.unsqueeze(axis)
                shape = list(ap.shape)
                shape[axis] = n
                return ap.broadcast_to(shape)

            v.memset(eps, EPS).then_inc(sem("dve"), 1)
            chain.n += 1
            dve.wait_ge(sem("silc"), 1)
            v.tensor_copy(condr, over(cc, 2, 32)).then_inc(sem("cond"), 1)

            def ada_out(a):
                dve.wait_ge(sem("ada"), 8 * a + 8)
                dve.wait_ge(sem("ab"), 64 * (a + 1))
                tt(MR[:, :], MR[:, :], PB[7 - 2 * (a % 2)][:, :], ALU.add).then_inc(sem("mr"), 1)

            def columns_out(a):
                l, gr = divmod(a, 3)
                dve.wait_ge(sem("mcp"), a + 1)
                for v_ in MOD_VECTORS[gr]:
                    last = v.tensor_copy(MODC[:, l, gr + v_ if gr < 2 else 3], PB[6][:, v_ * C:(v_ + 1) * C])
                last.then_inc(sem("mc"), 1)

            def gains(k):
                l, w = divmod(k, 2)
                dve.wait_ge(sem("mc"), 3 * l + 2 * w + 1)
                stt(GC[:, k], MODC[:, l, 2 * w + 1], 1.0, NRM[:, w, l], ALU.add, ALU.mult).then_inc(sem("gc"), 1)

            def normalise_x(k, t):
                dve.wait_ge(sem("sd"), 4 * k + t + 1)
                link(v.reciprocal(rs[:, t:t + 1], sd[:, t:t + 1]))
                ts(XN[:, t, :].rearrange("p (c m) -> p c m", c=C), X[:, t, :].rearrange("p (m c) -> p c m", c=C),
                   rs[:, t:t + 1], None, ALU.mult).then_inc(sem("xn"), 1)

            def modulate(k, t):
                l, w = divmod(k, 2)
                dve.wait_ge(sem("gc"), k + 1)
                dve.wait_ge(sem("xt"), 4 * k + t + 1)
                if k == 2:
                    dve.wait_ge(sem("comb"), 2)
                for c in range(C // 2, C):
                    last = ts(HT[:, c, t * P:(t + 1) * P], PB[2 * t + 1][:, (c - 4) * P:(c - 3) * P], GC[:, k, c:c + 1],
                              MODC[:, l, 2 * w, c:c + 1], ALU.mult, ALU.add)
                last.then_inc(sem("hD"), 1)

            def norm(k, update):
                for t in range(T):
                    update((k - 1) // 2, t)
                    normalise_x(k, t)
                    if t:
                        modulate(k, t - 1)
                modulate(k, T - 1)

            def da_project():
                def step(hb, n12, n):
                    w, t = divmod(n12, T)
                    if w == 2:
                        return
                    m = hb * 8 + n12
                    b = m % 2
                    dve.wait_ge(sem("dsq"), m + 1)
                    wait(dve, sem("dsd"), m - 1)
                    red(hss[:, b, 0:8], SQ.rearrange("p (h x) -> p h x", h=8), AX.X, ALU.add).then_inc(sem("dss"), 1)
                    dve.wait_ge(sem("dsd"), m + 1)
                    wait(dve, sem("day"), m)
                    v.reciprocal(hrs[:, b, 0:8], hsd[:, b, 0:8]).then_inc(sem("drs"), 1)
                    dve.wait_ge(sem("drs"), m + 1)
                    wait(dve, sem("dat"), m)
                    src = PB[n % 4][:, :].rearrange("p (h x) -> p h x", h=8)
                    m1, m2 = view(M1, 0, 8, DH), view(M2, 0, 8, DH)
                    cos, sin = DT[:, t, 2 * w], DT[:, t, 2 * w + 1]
                    nn = DH // 2
                    tt(m1, src, over(cos, 1, 8), ALU.mult)
                    tt(m2[:, :, 0:nn], src[:, :, nn:], over(sin[:, 0:nn], 1, 8), ALU.mult)
                    wait(dve, sem("daev"), n)
                    tt(m2[:, :, nn:], src[:, :, 0:nn], over(sin[:, nn:], 1, 8), ALU.mult).then_inc(sem("daev"), 1)
                    dve.wait_ge(sem("daev"), n + 1)
                    link(tt(m1, m1, m2, ALU.add))
                    tt(YT.rearrange("p (h x) -> p h x", h=8), m1, over(hrs[:, b, 0:8], 2, DH),
                       ALU.mult).then_inc(sem("day"), 1)

                for n in range(24):
                    step(*divmod(n, 12), n)
                    for u in ada_after(n):
                        if u % C == 0 and u > AHEAD:
                            columns_out(u // C - 1)
                        if u % C == C - 1:
                            ada_out(u // C)
                columns_out(5)

            def maxima(l, i, pair):
                t, b, n = i % T, i % 2, 32 * l + i
                L = (t + 1) * P
                dve.wait_ge(sem("sc"), n + 1)
                wait(dve, sem("exp"), n - 1)
                wait(dve, sem("nm"), n - 1)
                for a in range(2):
                    last = red(mx[:, b, a:a + 1], PB[2 * pair + a][:, 0:L], AX.X, ALU.max)
                link(last)
                ts(nmx[:, b], mx[:, b], -((DH, QK)[l] ** -0.5), None, ALU.mult).then_inc(sem("nm"), 1)

            def da_attention():
                def normalise(i):
                    t, b = i % T, i % 2
                    L = (t + 1) * P
                    dve.wait_ge(sem("exp"), i + 1)
                    wait(dve, sem("p"), i)
                    link(v.reciprocal(ls[:, b], ls[:, b]))
                    ts(rl[:, b, 1:2], ls[:, b, 1:2], lam[:, 3:4], None, ALU.mult)
                    link(ts(pr[b][:, 0, 0:L], pr[b][:, 0, 0:L], ls[:, b, 0:1], None, ALU.mult))
                    stt(pr[b][:, 0, 0:L], pr[b][:, 1, 0:L], rl[:, b, 1:2], pr[b][:, 0, 0:L], ALU.mult,
                        ALU.add).then_inc(sem("p"), 1)

                maxima(0, 0, 0)
                maxima(0, 1, 1)
                for i in range(32):
                    normalise(i)
                    if i + 2 < 32:
                        maxima(0, i + 2, i % 2)

            def output_norm():
                for t in range(T):
                    o = slice(8 * t, 8 * t + 8)
                    dve.wait_ge(sem("osq"), t + 1)
                    red(hss[:, 0, o], view(PS, 0, DA_H, P), AX.X, ALU.add).then_inc(sem("oss"), 1)
                    dve.wait_ge(sem("osd"), t + 1)
                    link(v.reciprocal(hrs[:, 0, o], hsd[:, 0, o]))
                    ot = OTOK[:, t, :].rearrange("p (h x) -> p h x", h=DA_H)
                    tt(ot, ot, over(hrs[:, 0, o], 2, P), ALU.mult).then_inc(sem("on"), 1)

            def residual(l, t):
                for n in range(2):
                    m = 8 * l + 2 * t + n
                    dve.wait_ge(sem("wo"), m + 1)
                    tmp = view(PS, 1024 + NH * n, NH)
                    cols = slice(n * NH, (n + 1) * NH)
                    tt(tmp, PB[2 * t + n][:, :], GM[:, cols], ALU.mult).then_inc(sem("oev"), 1)
                    dve.wait_ge(sem("oev"), m + 1)
                    last = tt(X[:, t, cols], X[:, t, cols], tmp, ALU.add)
                last.then_inc(sem("res"), 1)
                dve.wait_ge(sem("res"), 4 * l + t + 1)

            def first_max(oh, s, width, iota_, tmp):
                m, cand = tmp
                link(red(m, s, AX.X, ALU.max))
                link(tt(oh, s, over(m, 2, width), ALU.is_ge))
                link(stt(cand, oh, -100.0, over(iota_, 1, T), ALU.mult, ALU.add))
                link(red(m, cand, AX.X, ALU.min))
                link(tt(oh, cand, over(m, 2, width), ALU.is_equal))

            def gate(l):
                at = [0]

                def r(*shape):
                    x = view(SCR, at[0], *shape)
                    at[0] += math.prod(shape)
                    return x

                gl = view(SCR, 0, T, G)
                M = view(SCR, 256, T, E)
                el = view(SCR, 512, T, EPG)
                at[0] = 640
                m4, gb, ohg, cg = r(T), r(T, G), r(T, G), r(T, G)
                gate_, br, es, cand, oh1, oh2, tmp8 = r(T), r(T, EPG), r(T, EPG), r(T, EPG), r(T, EPG), r(T, EPG), r(T, EPG)
                s1 = r(T)
                LG = r(T, NR)
                sel = r(T * EPG, G)
                OH = r(T, 2, E)
                tmp = r(T, 2, E)
                rank, slot, slotf = r(T, E), r(T, E), r(2 * T)
                cnt, extra, cum, incl, base, ge = r(E), r(E), r(E), r(2, E), r(E), r(T, E)
                step1, empty = r(2 * T), r(NPAIR)
                cmp = r(E, LEVELS)
                tailf = r(1 + TAILS)
                assert at[0] <= 2560
                dve.wait_ge(sem("lg"), 4 * (l + 1))
                dve.wait_ge(sem("bgr"), 32 * (l + 1))
                dve.wait_ge(sem("iota"), l + 1)
                link(v.tensor_copy(LG, PB[0][:, 0:T * NR].rearrange("p (t n) -> p t n", t=T)))
                link(red(m4, LG[:, :, 0:G], AX.X, ALU.max))
                tt(gl, LG[:, :, 0:G], over(m4, 2, G), ALU.subtract).then_inc(sem("gl"), 1)
                dve.wait_ge(sem("gle"), l + 1)
                link(red(m4, gl, AX.X, ALU.add))
                link(v.reciprocal(m4, m4))
                link(tt(gl, gl, over(m4, 2, G), ALU.mult))
                link(tt(gb, gl, over(bgr[:, 0:G], 1, T), ALU.add))
                first_max(ohg, gb, G, i8[:, 0:G], (m4, cg))
                link(tt(cg, gl, ohg, ALU.mult))
                link(red(gate_, cg, AX.X, ALU.add))
                sel4 = sel.rearrange("p (t e) g -> p t e g", t=T)
                link(tt(sel4, LG[:, :, G:].rearrange("p t (g e) -> p t e g", g=G), over(ohg, 2, EPG), ALU.mult))
                link(red(el, sel4, AX.X, ALU.add))
                link(tt(sel4, over(bgr[:, G:].rearrange("p (g e) -> p e g", g=G), 1, T), over(ohg, 2, EPG), ALU.mult))
                link(red(br, sel4, AX.X, ALU.add))
                link(red(m4, el, AX.X, ALU.max))
                tt(el, el, over(m4, 2, EPG), ALU.subtract).then_inc(sem("el"), 1)
                dve.wait_ge(sem("ele"), l + 1)
                link(red(m4, el, AX.X, ALU.add))
                link(v.reciprocal(m4, m4))
                link(tt(el, el, over(m4, 2, EPG), ALU.mult))
                link(tt(es, el, br, ALU.add))
                first_max(oh1, es, EPG, i8, (m4, cand))
                link(stt(es, oh1, NEG, es, ALU.mult, ALU.add))
                first_max(oh2, es, EPG, i8, (m4, cand))
                for k, oh in enumerate((oh1, oh2)):
                    for g in range(G):
                        last = tt(OH[:, :, k, g * EPG:(g + 1) * EPG], oh, over(ohg[:, :, g], 2, EPG), ALU.mult)
                v.memset(MS[:, 0], 0.0)
                link(last)
                link(tt(M, OH[:, :, 0], OH[:, :, 1], ALU.add))
                for t in range(T):
                    last = tt(MS[:, t + 1], MS[:, t], M[:, t], ALU.add)
                    if t < T - 1:
                        link(last)
                last.then_inc(sem("M"), 1)
                for k, oh in enumerate((oh1, oh2)):
                    link(tt(tmp8, el, oh, ALU.mult))
                    link(red(Wt[:, :, k], tmp8, AX.X, ALU.add))
                link(tt(s1, Wt[:, :, 0], Wt[:, :, 1], ALU.add))
                link(v.reciprocal(s1, s1))
                link(tt(s1, s1, gate_, ALU.mult))
                link(tt(Wt, Wt, over(s1, 2, 2), ALU.mult))
                dve.wait_ge(sem("rank"), l + 1)
                link(v.tensor_copy(rank, PB[1][:, 0:T * E].rearrange("p (t e) -> p t e", t=T)))
                link(v.tensor_copy(cnt, PB[1][:, T * E:(T + 1) * E]))
                link(tt(cmp, over(cnt, 2, LEVELS), over(th, 1, E), ALU.is_gt))
                link(red(extra, cmp, AX.X, ALU.add))
                cur = extra
                for k in range(5):
                    sh, new = 1 << k, incl[:, k % 2]
                    v.tensor_copy(new[:, 0:sh], cur[:, 0:sh])
                    link(tt(new[:, sh:], cur[:, sh:], cur[:, 0:E - sh], ALU.add))
                    cur = new
                link(tt(cum, cur, extra, ALU.subtract))
                link(ts(base, cum, float(OVER), float(E * CAP - CAP), ALU.mult, ALU.add))
                link(stt(base, i32f, -float(CAP), base, ALU.mult, ALU.add))
                link(ts(ge, rank, float(CAP), None, ALU.is_ge))
                link(tt(ge, ge, over(base, 1, T), ALU.mult))
                link(tt(slot, rank, ge, ALU.add))
                link(ts(base, i32f, float(CAP), None, ALU.mult))
                link(tt(slot, slot, over(base, 1, T), ALU.add))
                link(tt(tmp, OH, over(slot, 2, 2), ALU.mult))
                link(red(slotf, tmp.rearrange("p t k e -> p (t k) e"), AX.X, ALU.add))
                ge8 = tmp.rearrange("p t k e -> p (t k) e")
                link(tt(ge8, over(slotf, 2, NPAIR), over(starts, 1, 2 * T), ALU.is_ge))
                link(red(step1, ge8, AX.X, ALU.add))
                link(stt(slotf, step1, -float(P), slotf, ALU.mult, ALU.add))
                link(ts(slotf, slotf, float(P), None, ALU.add))
                link(tt(hotn, over(step1, 2, NPAIR), over(steps1, 1, 2 * T), ALU.is_equal))
                link(tt(hotn, hotn, over(pair1.rearrange("p t k -> p (t k)"), 2, NPAIR), ALU.mult))
                tt(hotp, over(slotf, 2, P), over(iota_p, 1, 2 * T), ALU.is_equal).then_inc(sem("hot"), 1)
                dve.wait_ge(sem("tab"), l + 1)
                link(ts(empty, PB[2][:, 0:NPAIR], 0.0, float(NOWHERE), ALU.is_equal, ALU.mult))
                link(stt(idx[:, 0, :], PB[2][:, 0:NPAIR], -1.0, empty, ALU.add, ALU.add))
                ts(idx[:, 1, :], idx[:, 0, :], 1, None, ALU.logical_shift_right).then_inc(sem("idx"), 1)
                o16 = view(SCR, 2816, TAILS, E)
                o16b = view(SCR, 2816 + TAILS * E, TAILS, E)
                link(tt(o16, over(i16f, 2, E), over(cum, 1, TAILS), ALU.is_ge))
                link(tt(o16b, over(i16f, 2, E), over(cur, 1, TAILS), ALU.is_lt))
                link(tt(o16, o16, o16b, ALU.mult))
                link(tt(o16, o16, over(i32f, 1, TAILS), ALU.mult))
                link(red(tailf[:, 1:], o16, AX.X, ALU.add))
                link(v.tensor_copy(tailf[:, 0:1], cur[:, E - 1:E]))
                v.tensor_copy(CTL[:, :], tailf[0:1, :]).then_inc(sem("ctl"), 1)

            def modulate_rows(l, b, n, before):
                dve.wait_ge(sem(f"xt{l}"), n + 1)
                wait(dve, sem(f"b{l}"), before)
                for c in range(1, C, 2):
                    last = ts(xgT[b][:, c, :], PB[1][:, (c // 2) * P:(c // 2 + 1) * P], GC[:, 2 * l + 1, c:c + 1],
                              MODC[:, l, 2, c:c + 1], ALU.mult, ALU.add)
                last.then_inc(sem(f"xD{l}"), 1)

            def hidden(l, n):
                dve.wait_ge(sem(f"b{l}"), n + 1)
                dve.wait_ge(sem(f"sil{l}"), n + 1)
                wait(dve, sem(f"ht{l}"), n)
                tt(hid, sil.rearrange("p (m c) -> p c m", c=2), PB[3][:, 0:FF].rearrange("p (m c) -> p c m", c=2),
                   ALU.mult).then_inc(sem(f"hid{l}"), 1)

            def rows_out(l, b, q, n):
                dve.wait_ge(sem(f"y{l}"), n + 1)
                wait(dve, sem(f"scat{l}{b}"), 16 * q)
                for m in range(2):
                    cols = slice(m * NH, (m + 1) * NH)
                    last = tt(ysb[b][:, cols], PB[5 + m][:, :], GF[:, cols], ALU.mult)
                last.then_inc(sem(f"yD{l}"), 1)

            def experts(l):
                dve.wait_ge(sem(f"gf{l}"), 16)

                def step(i, b, n, more=True):
                    hidden(l, n)
                    if more:
                        modulate_rows(l, 1 - b, n + 1, n)
                    rows_out(l, b, i, n)

                modulate_rows(l, 0, 0, 0)
                step(0, 0, 0)
                step(0, 1, 1)
                with dve.Fori(1, PAIRS // 2 - 1) as i:
                    for b in range(2):
                        step(i, b, 2 * i + b)
                step(PAIRS // 2 - 1, 0, PAIRS - 2)
                step(PAIRS // 2 - 1, 1, PAIRS - 1, more=False)
                dve.wait_ge(sem("ctl"), l + 1)
                tails = dve.value_load(CTL[0:1, 0:1], min_val=0, max_val=TAILS)

                def overflow(i, b):
                    n = PAIRS + 2 * i + b
                    modulate_rows(l, b, n, n - 1)
                    step(PAIRS // 2 + i, b, n, more=False)
                overflow_steps(dve, tails, overflow)

            def combine(l, t):
                dve.wait_ge(sem(f"yl{t}"), 16 * (l + 1))
                y = YP[t]
                link(stt(X[:, t, :], y[:, 0], Wt[:, t, 0:1], X[:, t, :], ALU.mult, ALU.add))
                stt(X[:, t, :], y[:, 1], Wt[:, t, 1:2], X[:, t, :], ALU.mult, ALU.add).then_inc(sem("comb"), 1)
                dve.wait_ge(sem("comb"), 4 * l + t + 1)

            def latents():
                for t in range(T):
                    o = [PB[2 * (t % 2)], PB[2 * (t % 2) + 1]]
                    dve.wait_ge(sem("lsd"), t + 1)
                    v.reciprocal(rs[:, 4:7], sd[:, 4:7]).then_inc(sem("lrs"), 1)
                    dve.wait_ge(sem("lrs"), t + 1)
                    wait(dve, sem("ltt"), t)
                    ts(LT_[:, 0:QR], o[0][:, 0:QR], rs[:, 4:5], None, ALU.mult)
                    ts(LT_[:, QR:], o[1][:, 0:KVR], rs[:, 5:6], None, ALU.mult).then_inc(sem("ln"), 1)
                    src = o[1][:, KVR:KVR + ROPE].unsqueeze(1)
                    rotate2(KP[:, t, :], src, RT[:, t, 2], RT[:, t, 3], t)
                    if t:
                        turn_latents(t - 1)
                turn_latents(T - 1)

            def rotate2(dst, src, cos, sin, t):
                n = ROPE // 2
                m1, m2 = view(PS, 2048, 1, ROPE), view(PS, 2048 + ROPE, 1, ROPE)
                tt(m1, src, over(cos, 1, 1), ALU.mult)
                tt(m2[:, :, 0:n], src[:, :, n:], over(sin[:, 0:n], 1, 1), ALU.mult)
                tt(m2[:, :, n:], src[:, :, 0:n], over(sin[:, n:], 1, 1), ALU.mult).then_inc(sem("lev"), 1)
                dve.wait_ge(sem("lev"), t + 1)
                link(tt(m1, m1, m2, ALU.add))
                link(ts(dst, m1[:, 0], rs[:, 6:7], None, ALU.mult))

            def turn_latents(t):
                dve.wait_ge(sem("ltt"), t + 1)
                for k in range(KVC):
                    last = ts(CT[:, QRC + k, t * P:(t + 1) * P], PB[5][:, k * P:(k + 1) * P], kvan[:, k:k + 1], None, ALU.mult)
                last.then_inc(sem("ltevD"), 1)

            def mla():
                def sums(n):
                    b = n % 2
                    sq, sk = view(PS, 0, 4, QK), view(PS, 4 * QK, 4, NOPE)
                    dve.wait_ge(sem("msq"), n + 1)
                    wait(dve, sem("msd"), n - 1)
                    red(hss[:, b, 0:4], sq[:, :, 0:NOPE], AX.X, ALU.add)
                    red(hss[:, b, 8:12], sq[:, :, NOPE:], AX.X, ALU.add)
                    red(hss[:, b, 4:8], sk, AX.X, ALU.add).then_inc(sem("mss"), 1)

                def heads(n):
                    t, b = n % T, n % 2
                    q = PB[2 * b][:, 0:4 * QK].rearrange("p (h x) -> p h x", h=4)
                    kv = PB[2 * b + 1][:, :].rearrange("p (h x) -> p h x", h=4)
                    dve.wait_ge(sem("mrs"), n + 1)
                    wait(dve, sem("mt"), n - 1)
                    nn = ROPE // 2
                    m1, m2 = view(PS, 2048, 4, ROPE), view(PS, 2048 + 128, 4, ROPE)
                    qp = q[:, :, NOPE:]
                    cos, sin = RT[:, t, 0], RT[:, t, 1]
                    tt(QY[b][:, :, 0:NOPE], q[:, :, 0:NOPE], over(hrs[:, b, 0:4], 2, NOPE), ALU.mult)
                    tt(KY[b][:, :, 0:NOPE], kv[:, :, 0:NOPE], over(hrs[:, b, 4:8], 2, NOPE), ALU.mult)
                    tt(m1, qp, over(cos, 1, 4), ALU.mult)
                    tt(m2[:, :, 0:nn], qp[:, :, nn:], over(sin[:, 0:nn], 1, 4), ALU.mult)
                    tt(m2[:, :, nn:], qp[:, :, 0:nn], over(sin[:, nn:], 1, 4), ALU.mult).then_inc(sem("mev"), 1)
                    v.tensor_copy(KY[b][:, :, NOPE:], over(KP[:, t, :], 1, 4))
                    dve.wait_ge(sem("mev"), n + 1)
                    link(tt(m1, m1, m2, ALU.add))
                    tt(QY[b][:, :, NOPE:], m1, over(hrs[:, b, 8:12], 2, ROPE), ALU.mult).then_inc(sem("my"), 1)

                def keys_out(n):
                    hb, t = divmod(n, T)
                    dve.wait_ge(sem("mt"), n + 1)
                    wait(dve, sem("sc"), 32 + 8 * max(hb - 2, 0))
                    ts(mk[hb % 3][0:QK, :, t * P:(t + 1) * P], PB[5][0:QK, :].rearrange("p (h q) -> p h q", h=4),
                       knc[0:QK, :], None, ALU.mult).then_inc(sem("mtevD"), 1)

                def inverses(i):
                    b, n = i % 2, 32 + i
                    dve.wait_ge(sem("exp"), n + 1)
                    wait(dve, sem("oe"), n - 1)
                    v.reciprocal(rl[:, b], ls[:, b]).then_inc(sem("p"), 1)

                def probabilities_out(i):
                    t, b, n = i % T, i % 2, 32 + i
                    L = (t + 1) * P
                    dve.wait_ge(sem("tr"), n + 1)
                    wait(dve, sem("av"), n - 1)
                    v.tensor_copy(aT[b][:, 1, 0:L], PB[5][:, 0:L]).then_inc(sem("tev1"), 1)

                def output(i):
                    (g, t), b, n = divmod(i, T), i % 2, 32 + i
                    dve.wait_ge(sem("av"), n + 1)
                    tt(OTOK[:, t, g * P:(g + 1) * P].rearrange("p (a x) -> p a x", a=2),
                       PB[6 + b][:, 0:P].rearrange("p (a x) -> p a x", a=2), over(rl[:, b], 2, VD),
                       ALU.mult).then_inc(sem("oe"), 1)

                def project_part(n0, n1):
                    for n in range(n0, n1):
                        sums(n)
                        if n >= n0 + 2:
                            keys_out(n - 2)
                        heads(n)
                    keys_out(n1 - 2)
                    keys_out(n1 - 1)

                def attention_part(i0, i1):
                    maxima(1, i0, 0)
                    maxima(1, i0 + 1, 1)
                    for i in range(i0, i1):
                        inverses(i)
                        if i + 2 < i1:
                            maxima(1, i + 2, i % 2)
                        probabilities_out(i)
                        if i > i0:
                            output(i - 1)
                    output(i1 - 1)

                for part, first, end in MLA_PARTS:
                    (project_part if part == "project" else attention_part)(first, end)

            def tables():
                lp = view(SCR, 2560, 2, DH)
                link(tt(lp, lamv[:, 0:4:2], lamv[:, 1:4:2], ALU.mult))
                red(lam[:, 0:2], lp, AX.X, ALU.add).then_inc(sem("lams"), 1)
                ang, kk = view(SCR, 1280, T, 48), view(SCR, 1536, T, 48)
                link(v.tensor_copy(posf, posi[:, :]))
                link(tt(ang, over(posf, 2, 48), over(invs, 1, T), ALU.mult))
                link(ts(kk, ang, 1.0 / TWO_PI, None, ALU.mult))
                link(ts(kk, kk, MAGIC, None, ALU.add))
                link(ts(kk, kk, MAGIC, None, ALU.subtract))
                for part in (PI_A, PI_B, PI_C):
                    link(stt(ang, kk, -part, ang, ALU.mult, ALU.add))
                ts(ang, ang, math.pi * (1 - 1e-7), -math.pi * (1 - 1e-7), ALU.min, ALU.max).then_inc(sem("ang"), 1)
                dve.wait_ge(sem("lame"), 1)
                link(tt(lam[:, 2:3], lam[:, 1:2], lam[:, 0:1], ALU.subtract))
                link(ts(lam[:, 3:4], lam[:, 2:3], -LAMBDA_INIT, None, ALU.add))
                link(ts(subc, subc, 1.0 - LAMBDA_INIT, None, ALU.mult))
                dve.wait_ge(sem("sin"), 1)
                sn, cs = view(SCR, 2048, T, 48), view(SCR, 2304, T, 48)
                link(tt(cs, cs, cs, ALU.mult))
                link(ts(cs, cs, -2.0, 1.0, ALU.mult, ALU.add))
                for tab, half_dim, at, g0 in ((DT, DH // 2, 0, 0), (RT, ROPE // 2, DH // 2, 2 * DH)):
                    n = half_dim
                    for w in range(2):
                        g1 = gnb[:, g0 + 2 * n * w:g0 + 2 * n * w + n]
                        g2 = gnb[:, g0 + 2 * n * w + n:g0 + 2 * n * (w + 1)]
                        si, co = sn[:, :, at:at + n], cs[:, :, at:at + n]
                        tt(tab[:, :, 2 * w, 0:n], co, over(g1, 1, T), ALU.mult)
                        tt(tab[:, :, 2 * w, n:], co, over(g2, 1, T), ALU.mult)
                        link(tt(tab[:, :, 2 * w + 1, 0:n], si, over(g2, 1, T), ALU.mult))
                        tt(tab[:, :, 2 * w + 1, n:], si, over(g1, 1, T), ALU.mult)
                        link(ts(tab[:, :, 2 * w + 1, 0:n], tab[:, :, 2 * w + 1, 0:n], -1.0, None, ALU.mult))

            for t in range(T):
                normalise_x(0, t)
            dve.wait_ge(sem("in"), 16 * N_IN)
            ada_out(0)
            columns_out(0)
            gains(0)
            for t in range(T):
                modulate(0, t)
            tables()
            da_project()
            gains(1)
            da_attention()
            output_norm()
            dve.wait_ge(sem("gm0"), 16)
            norm(1, residual)
            gate(0)
            experts(0)
            gains(2)
            norm(2, combine)
            latents()
            mla()
            gains(3)
            dve.wait_ge(sem("gm1"), 16)
            norm(3, residual)
            gate(1)
            experts(1)
            for t in range(T):
                combine(1, t)

        @block.gpsimd
        def _(pool):
            g = nc.gpsimd

            def bias_rows(a):
                l, gr = divmod(a, 3)
                for j in range(4):
                    n = (4 * gr + j) * NH
                    pool.dma_start(MR[32 * j:32 * j + 32, :], A["ada_b"][l, n:n + NH].partition_broadcast(32)).then_inc(sem("ab"), 16)

            bias_rows(0)
            g.memset(ones[:, :], 1.0)
            g.memset(ident[:, :], 0.0)
            g.memset(mneg[:, :], 0.0)
            g.memset(tri[:, :], 1.0).then_inc(sem("pool"), 1)
            pool.wait_ge(sem("pool"), 1)
            g.affine_select(out=ident[:, :], in_=ident[:, :], compare_op=ALU.not_equal, fill=1.0, base=0,
                            pattern=[[-1, P]], channel_multiplier=1).then_inc(sem("const"), 1)
            g.affine_select(out=tri[:, :], in_=tri[:, :], compare_op=ALU.is_gt, fill=0.0, base=0,
                            pattern=[[1, P]], channel_multiplier=-1).then_inc(sem("const"), 1)
            g.affine_select(out=mneg[:, :], in_=mneg[:, :], compare_op=ALU.is_ge, fill=NEG, base=0,
                            pattern=[[-1, P]], channel_multiplier=1).then_inc(sem("const"), 1)
            g.iota(i8, [[1, EPG]], base=0, channel_multiplier=0, allow_small_or_imprecise_dtypes=True)
            g.iota(i32f, [[1, E]], base=0, channel_multiplier=0, allow_small_or_imprecise_dtypes=True)
            g.iota(i16f, [[1, TAILS]], base=0, channel_multiplier=0, allow_small_or_imprecise_dtypes=True)
            g.iota(th, [[OVER, LEVELS]], base=CAP, channel_multiplier=0, allow_small_or_imprecise_dtypes=True).then_inc(sem("pool"), 1)
            pool.wait_ge(sem("pool"), 2)
            g.memset(qnc[NOPE:QK, :], 1.0)
            g.memset(knc[NOPE:QK, :], 1.0).then_inc(sem("pool"), 1)
            def router_weights(l):
                with nc.allow_non_contiguous_dma(reason="narrow router weights"):
                    pool.dma_start(WGR[:, :, 0:G], A["moe_w_group"][l].rearrange("(p c) n -> p c n", c=C)).then_inc(sem("wgr"), 16)
                    pool.dma_start(WGR[:, :, G:], A["moe_w_router"][l].rearrange("(p c) n -> p c n", c=C)).then_inc(sem("wgr"), 16)
                    pool.dma_start(bgr[:, 0:G], A["moe_b_group"][l].partition_broadcast(P)).then_inc(sem("bgr"), 16)
                    pool.dma_start(bgr[:, G:], A["moe_b_router"][l].rearrange("g e -> (g e)").partition_broadcast(P)).then_inc(sem("bgr"), 16)

            def gate_row(l, w):
                dst, s = (GM, f"gm{l}") if w == 2 else (GF, f"gf{l}")
                pool.dma_start(dst[:, :], mod_d[l, w * D:(w + 1) * D].partition_broadcast(P)).then_inc(sem(s), 16)

            def mod_group(a):
                l, gr = divmod(a, 3)
                pool.wait_ge(sem("mr"), a + 1)
                if gr:
                    pool.dma_start(mod_d[l, gr * 2 * D:(gr + 1) * 2 * D].rearrange("(j n) -> j n", j=4),
                                   MR[0:P:32, :]).then_inc(sem("mo"), 16)
                    pool.wait_ge(sem("mo"), 16 * (2 * l + gr))
                pool.wait_ge(sem("mcp"), a + 1)
                if a < 5:
                    bias_rows(a + 1)
                if l == 0 and gr:
                    gate_row(0, 3 * gr - 1)

            last_token, last_pair = pool.to_reg(S - 1), pool.to_reg(2 * S - 1)
            pool.wait_ge(sem("pool"), 3)
            g.memset(dak[0][64:P, :, :], 0.0).then_inc(sem("pool"), 1)
            pool.wait_ge(sem("pool"), 4)
            g.memset(dak[1][0:64, :, :], 0.0).then_inc(sem("pool"), 1)
            pool.wait_ge(sem("pool"), 5)
            router_weights(0)
            for a in range(6):
                mod_group(a)

            def settle():
                pool.sem_inc(sem("pool_turns"), 1)

            def layer(l):
                pool.wait_ge(sem("av"), 32 * (l + 1))
                g.iota(iota_p, [[1, P]], base=0, channel_multiplier=0, allow_small_or_imprecise_dtypes=True)
                g.iota(starts, [[P, NPAIR]], base=0, channel_multiplier=0, allow_small_or_imprecise_dtypes=True)
                g.iota(steps1, [[1, NPAIR]], base=1, channel_multiplier=0, allow_small_or_imprecise_dtypes=True)
                g.iota(pair1, [[2 * P, T], [1, 2]], base=1, channel_multiplier=2,
                       allow_small_or_imprecise_dtypes=True).then_inc(sem("iota"), 1)
                for t in range(T):
                    pool.wait_ge(sem("xn"), 4 * (2 * l + 1) + t + 1)
                    pool.dma_start(xn_d[l][t * P:(t + 1) * P, :], XN[:, t, :]).then_inc(sem("xd"), 16)
                if l == 0:
                    gate_row(1, 2)
                def gather(b, q, n, before):
                    wait(pool, sem(f"xt{l}"), before)
                    wait(pool, sem(f"gath{l}{b}"), 16 * q)
                    pool.wait_ge(sem("idx"), l + 1)
                    g.tensor_copy(ci[:, b:b + 1], idx[:, 1, bass.ds(n, 1)]).then_inc(sem(f"gi{l}"), 1)
                    pool.wait_ge(sem(f"gi{l}"), n + 1)
                    settle()
                    pool.wait_ge(sem("xd"), 16 * T * (l + 1))
                    pool.indirect_dma_start(xg[b], None, xn_d[l][:, :],
                                            bass.IndirectOffsetOnAxis(ap=ci[:, b:b + 1], axis=0), bounds_check=last_token,
                                            oob_is_err=False).then_inc(sem(f"gath{l}{b}"), 16)

                def scatter(b, q, n):
                    wait(pool, sem(f"scat{l}{b}"), 16 * q)
                    pool.wait_ge(sem("idx"), l + 1)
                    g.tensor_copy(ci[:, 2 + b:3 + b], idx[:, 0, bass.ds(n, 1)]).then_inc(sem(f"si{l}"), 1)
                    pool.wait_ge(sem(f"si{l}"), n + 1)
                    pool.wait_ge(sem(f"yD{l}"), n + 1)
                    settle()
                    pool.indirect_dma_start(y_d[l][:, :], bass.IndirectOffsetOnAxis(ap=ci[:, 2 + b:3 + b], axis=0),
                                            ysb[b], None, bounds_check=last_pair, oob_is_err=False).then_inc(sem(f"scat{l}{b}"), 16)

                def turn(i):
                    for b in range(2):
                        gather(b, i + 1, 2 * i + 2 + b, 2 * i + b + 1)
                        scatter(b, i, 2 * i + b)

                half = PAIRS // 2
                for b in range(2):
                    gather(b, 0, b, 0)
                turn(0)
                with pool.Fori(1, half - 1) as i:
                    turn(i)
                for b in range(2):
                    scatter(b, half - 1, PAIRS - 2 + b)
                pool.wait_ge(sem("ctl"), l + 1)
                tails = pool.value_load(CTL[0:1, 0:1], min_val=0, max_val=TAILS)

                def overflow(i, b):
                    gather(b, half + i, PAIRS + 2 * i + b, PAIRS + 2 * i + b - 1)
                    scatter(b, half + i, PAIRS + 2 * i + b)
                    pool.wait_ge(sem(f"scat{l}{b}"), 16 * (half + i) + 16)
                    settle()
                overflow_steps(pool, tails, overflow)
                for b in range(2):
                    pool.wait_ge(sem(f"scat{l}{b}"), 16 * half)
                for t in range(T):
                    pool.dma_start(YP[t], y_d[l][2 * t * P:2 * (t + 1) * P, :]
                                   .rearrange("(p k) n -> p k n", k=2)).then_inc(sem(f"yl{t}"), 16)
                if l == 0:
                    router_weights(1)
                    pool.wait_ge(sem("comb"), T)
                    gate_row(1, 5)

            layer(0)
            layer(1)


N_IN = 18

_INS = ["x", "c", "positions", "ada_w", "ada_b", "norm_mix", "norm_ffn", "da_w_qkv", "da_q_norm", "da_k_norm",
        "da_lambda_q1", "da_lambda_k1", "da_lambda_q2", "da_lambda_k2", "da_subln", "da_w_o", "mla_w_in",
        "mla_q_a_norm", "mla_kv_a_norm", "mla_w_uq", "mla_w_ukv", "mla_q_nope_norm", "mla_q_pe_norm",
        "mla_k_nope_norm", "mla_k_pe_norm", "mla_w_o", "moe_w_group", "moe_b_group", "moe_w_router",
        "moe_b_router", "moe_w1", "moe_w3", "moe_w2"]


def kernel(**inputs):
    import numpy as np
    import concourse.bacc as bacc
    from concourse.bass_utils import run_bass_kernel_spmd as run

    nc = bacc.Bacc("TRN2", target_bir_lowering=False, num_devices=1)
    arrays, A = {}, {}
    for name in _INS:
        a = np.ascontiguousarray(inputs[name])
        arrays["in_" + name] = a
        A[name] = nc.dram_tensor("in_" + name, a.shape, mybir.dt.from_np(a.dtype), kind="ExternalInput").ap()
    freqs = []
    for name, dim in (("inv_da", DH), ("inv_mla", ROPE)):
        a = (10000.0 ** (-np.arange(0, dim, 2, dtype=np.float64) / dim)).astype(np.float32)
        arrays[name] = a
        freqs.append(nc.dram_tensor(name, a.shape, F32, kind="ExternalInput").ap())
    out = nc.dram_tensor("out", [S, D], F32, kind="ExternalOutput").ap()
    build(nc, A, freqs[0], freqs[1], out)
    r = run(nc, [arrays], core_ids=[0])
    return r.results[0]["out"].reshape(1, S, D)
```
